# Optimizing a Trainium2 kernel written in Bass

```python
import math
import jax, jax.numpy as jnp
from jax import lax
import numpy as np

D_MODEL = 2048
BATCH = 1
SEQ = 256
DEPTH = 1

ATTN_WIDTH = D_MODEL // 2
ATTN_HEAD_DIM = 128
N_ATTN_HEADS = ATTN_WIDTH // ATTN_HEAD_DIM
SSM_WIDTH = D_MODEL - ATTN_WIDTH
SSM_HEAD_DIM = 64
N_SSM_HEADS = SSM_WIDTH // SSM_HEAD_DIM
N_SSM_GROUPS = 2
SSM_HEADS_PER_GROUP = N_SSM_HEADS // N_SSM_GROUPS
D_STATE = 128
SSM_CONV = 4
SSM_CHUNK = 256
SSM_CONV_CH = SSM_WIDTH + 2 * N_SSM_GROUPS * D_STATE
MOBA_BLOCK = 256
MOBA_TOPK = 3
MOBA_Q_CHUNK = 32
REL_BUCKETS = 32
REL_MAX_DIST = 128
FFN_DIM = 5632
FFN_CONV = 3
IN_COLS = 3 * ATTN_WIDTH + 2 * SSM_WIDTH + 2 * N_SSM_GROUPS * D_STATE + N_SSM_HEADS
EPS = 1e-6


def rms_norm(x, g):
    xf = x.astype(jnp.float32)
    y = xf * lax.rsqrt(jnp.mean(xf * xf, axis=-1, keepdims=True) + EPS)
    return (y * g.astype(jnp.float32)).astype(x.dtype)

def causal_dwconv(x, w, b):
    k = w.shape[0]
    y = lax.conv_general_dilated(x, w[:, None, :].astype(x.dtype), window_strides=(1,),
                                 padding=[(k - 1, 0)], dimension_numbers=('NWC', 'WIO', 'NWC'),
                                 feature_group_count=x.shape[-1])
    return y + b.astype(x.dtype)

def pad_seq(x, mult):
    p = (-x.shape[1]) % mult
    return jnp.pad(x, [(0, 0), (0, p)] + [(0, 0)] * (x.ndim - 2))

def rel_bucket(dist):
    n = jnp.maximum(dist, 0)
    max_exact = REL_BUCKETS // 2
    nf = jnp.maximum(n, max_exact).astype(jnp.float32)
    large = max_exact + (jnp.log(nf / max_exact) / math.log(REL_MAX_DIST / max_exact)
                         * (REL_BUCKETS - max_exact)).astype(jnp.int32)
    large = jnp.minimum(large, REL_BUCKETS - 1)
    return jnp.where(n < max_exact, n, large)

def gather_blocks(blocks, sel):
    return jax.vmap(jax.vmap(lambda kb, s: kb[s]))(blocks, sel)

def moba_attention(q, k, v, rel_bias):
    bsz, s = q.shape[:2]
    q, k, v = [pad_seq(t, MOBA_BLOCK).transpose(0, 2, 1, 3) for t in (q, k, v)]
    sp = q.shape[2]
    nb = sp // MOBA_BLOCK
    n_sel = min(MOBA_TOPK, nb - 1)
    k_blocks = k.reshape(bsz, N_ATTN_HEADS, nb, MOBA_BLOCK, ATTN_HEAD_DIM)
    v_blocks = v.reshape(bsz, N_ATTN_HEADS, nb, MOBA_BLOCK, ATTN_HEAD_DIM)
    k_mean = jnp.mean(k_blocks, axis=3)
    scale = ATTN_HEAD_DIM ** -0.5
    bias_t = rel_bias.T.astype(jnp.float32)
    head_idx = jnp.arange(N_ATTN_HEADS)[:, None, None, None]

    def chunk(ci):
        q0 = ci * MOBA_Q_CHUNK
        blk = q0 // MOBA_BLOCK
        qc = lax.dynamic_slice_in_dim(q, q0, MOBA_Q_CHUNK, axis=2)
        q_pos = q0 + jnp.arange(MOBA_Q_CHUNK)
        k_own = lax.dynamic_index_in_dim(k_blocks, blk, axis=2, keepdims=False)
        v_own = lax.dynamic_index_in_dim(v_blocks, blk, axis=2, keepdims=False)
        dist_own = q_pos[:, None] - (blk * MOBA_BLOCK + jnp.arange(MOBA_BLOCK))[None, :]
        logit_own = (jnp.einsum('bhqd,bhkd->bhqk', qc, k_own).astype(jnp.float32) * scale
                     + bias_t[:, rel_bucket(dist_own)])
        logit_own = jnp.where(dist_own >= 0, logit_own, -jnp.inf)
        if n_sel == 0:
            p_own = jax.nn.softmax(logit_own, axis=-1).astype(v.dtype)
            return jnp.einsum('bhqk,bhkd->bhqd', p_own, v_own)
        gate = jnp.einsum('bhqd,bhnd->bhqn', qc, k_mean).astype(jnp.float32)
        gate = jnp.where(jnp.arange(nb) < blk, gate, -jnp.inf)
        _, sel = lax.top_k(gate, n_sel)
        k_sel = gather_blocks(k_blocks, sel)
        v_sel = gather_blocks(v_blocks, sel)
        sel_pos = sel[..., None] * MOBA_BLOCK + jnp.arange(MOBA_BLOCK)
        dist_sel = q_pos[:, None, None] - sel_pos
        logit_sel = (jnp.einsum('bhqd,bhqtkd->bhqtk', qc, k_sel).astype(jnp.float32) * scale
                     + bias_t[head_idx, rel_bucket(dist_sel)])
        slot_ok = (jnp.arange(n_sel) < blk)[:, None]
        logit_sel = jnp.where(slot_ok, logit_sel, -jnp.inf)
        logits = jnp.concatenate(
            [logit_sel.reshape(bsz, N_ATTN_HEADS, MOBA_Q_CHUNK, n_sel * MOBA_BLOCK), logit_own], axis=-1)
        p = jax.nn.softmax(logits, axis=-1).astype(v.dtype)
        p_sel = p[..., :n_sel * MOBA_BLOCK].reshape(bsz, N_ATTN_HEADS, MOBA_Q_CHUNK, n_sel, MOBA_BLOCK)
        p_own = p[..., n_sel * MOBA_BLOCK:]
        return (jnp.einsum('bhqtk,bhqtkd->bhqd', p_sel, v_sel)
                + jnp.einsum('bhqk,bhkd->bhqd', p_own, v_own))

    out = lax.map(chunk, jnp.arange(sp // MOBA_Q_CHUNK))
    out = out.transpose(1, 0, 3, 2, 4).reshape(bsz, sp, N_ATTN_HEADS * ATTN_HEAD_DIM)
    return out[:, :s]

def segsum(x):
    t = x.shape[-1]
    xe = jnp.broadcast_to(x[..., :, None], x.shape + (t,))
    xe = jnp.where(jnp.tril(jnp.ones((t, t), bool), -1), xe, 0.0)
    xs = jnp.cumsum(xe, axis=-2)
    return jnp.where(jnp.tril(jnp.ones((t, t), bool)), xs, -jnp.inf)

def ssd_mixer(xs, z, bmat, cmat, dt_raw, conv_w, conv_b, dt_bias, a_log, d_skip, norm_g):
    bsz, s = xs.shape[:2]
    gn = N_SSM_GROUPS * D_STATE
    xbc = jax.nn.silu(causal_dwconv(jnp.concatenate([xs, bmat, cmat], axis=-1), conv_w, conv_b))
    x_h = xbc[..., :SSM_WIDTH].reshape(bsz, s, N_SSM_HEADS, SSM_HEAD_DIM).astype(jnp.float32)
    bm = xbc[..., SSM_WIDTH:SSM_WIDTH + gn].astype(jnp.float32)
    cm = xbc[..., SSM_WIDTH + gn:].astype(jnp.float32)
    dt = jax.nn.softplus(dt_raw.astype(jnp.float32) + dt_bias.astype(jnp.float32))
    a = -jnp.exp(a_log.astype(jnp.float32))
    xdt = pad_seq(x_h * dt[..., None], SSM_CHUNK)
    adt = pad_seq(dt * a, SSM_CHUNK)
    bm, cm = pad_seq(bm, SSM_CHUNK), pad_seq(cm, SSM_CHUNK)
    sp = xdt.shape[1]
    nc = sp // SSM_CHUNK
    X = xdt.reshape(bsz, nc, SSM_CHUNK, N_SSM_GROUPS, SSM_HEADS_PER_GROUP, SSM_HEAD_DIM)
    A = adt.reshape(bsz, nc, SSM_CHUNK, N_SSM_GROUPS, SSM_HEADS_PER_GROUP).transpose(0, 3, 4, 1, 2)
    Bm = bm.reshape(bsz, nc, SSM_CHUNK, N_SSM_GROUPS, D_STATE)
    Cm = cm.reshape(bsz, nc, SSM_CHUNK, N_SSM_GROUPS, D_STATE)
    A_cs = jnp.cumsum(A, axis=-1)
    Lm = jnp.exp(segsum(A))
    y_diag = jnp.einsum('bclgn,bcsgn,bgrcls,bcsgrp->bclgrp', Cm, Bm, Lm, X)
    decay_states = jnp.exp(A_cs[..., -1:] - A_cs)
    states = jnp.einsum('bclgn,bgrcl,bclgrp->bcgrpn', Bm, decay_states, X)
    states = jnp.concatenate([jnp.zeros_like(states[:, :1]), states], axis=1)
    chunk_tot = jnp.pad(A_cs[..., -1], ((0, 0), (0, 0), (0, 0), (1, 0)))
    decay_chunk = jnp.exp(segsum(chunk_tot))
    new_states = jnp.einsum('bgrzc,bcgrpn->bzgrpn', decay_chunk, states)
    prev_states = new_states[:, :-1]
    y_off = jnp.einsum('bclgn,bcgrpn,bgrcl->bclgrp', Cm, prev_states, jnp.exp(A_cs))
    y = (y_diag + y_off).reshape(bsz, sp, N_SSM_HEADS, SSM_HEAD_DIM)[:, :s]
    y = y + d_skip.astype(jnp.float32)[:, None] * x_h
    y = y.reshape(bsz, s, SSM_WIDTH) * jax.nn.silu(z.astype(jnp.float32))
    yg = y.reshape(bsz, s, N_SSM_GROUPS, SSM_WIDTH // N_SSM_GROUPS)
    yg = yg * lax.rsqrt(jnp.mean(yg * yg, axis=-1, keepdims=True) + EPS)
    return (yg.reshape(bsz, s, SSM_WIDTH) * norm_g.astype(jnp.float32)).astype(xs.dtype)

def conv_ffn(h, w_up, conv_w, conv_b, w_down):
    u = causal_dwconv(h @ w_up, conv_w, conv_b)
    g, val = jnp.split(u, 2, axis=-1)
    return (jax.nn.silu(g) * val) @ w_down

def first_inputs(seed: int = 0) -> dict:
    key = jax.random.key(seed)
    ks = jax.random.split(key, 24)
    f32 = jnp.float32
    nrm = lambda k, shape, sc: jax.random.normal(k, shape, f32) * sc
    dt0 = jnp.exp(jax.random.uniform(ks[10], (DEPTH, N_SSM_HEADS), f32)
                  * (math.log(0.1) - math.log(0.001)) + math.log(0.001))
    return {
        'x': nrm(ks[0], (BATCH, SEQ, D_MODEL), 1.0),
        'c': nrm(ks[1], (BATCH, D_MODEL), 1.0),
        'w_ada': nrm(ks[2], (DEPTH, D_MODEL, 6 * D_MODEL), 0.5 * D_MODEL ** -0.5),
        'b_ada': nrm(ks[3], (DEPTH, 6 * D_MODEL), 0.01),
        'norm_mix_g': 1.0 + nrm(ks[4], (DEPTH, D_MODEL), 0.05),
        'w_in': nrm(ks[5], (DEPTH, D_MODEL, IN_COLS), D_MODEL ** -0.5),
        'rel_bias': nrm(ks[6], (REL_BUCKETS, N_ATTN_HEADS), 0.2),
        'attn_norm_g': 1.0 + nrm(ks[7], (DEPTH, ATTN_WIDTH), 0.05),
        'conv_ssm_w': nrm(ks[8], (DEPTH, SSM_CONV, SSM_CONV_CH), SSM_CONV ** -0.5),
        'conv_ssm_b': nrm(ks[9], (DEPTH, SSM_CONV_CH), 0.01),
        'dt_bias': dt0 + jnp.log(-jnp.expm1(-dt0)),
        'a_log': jnp.log(jax.random.uniform(ks[11], (DEPTH, N_SSM_HEADS), f32, 1.0, 16.0)),
        'd_skip': 1.0 + nrm(ks[12], (DEPTH, N_SSM_HEADS), 0.1),
        'ssm_norm_g': 1.0 + nrm(ks[13], (DEPTH, SSM_WIDTH), 0.05),
        'w_out': nrm(ks[14], (DEPTH, ATTN_WIDTH + SSM_WIDTH, D_MODEL), (ATTN_WIDTH + SSM_WIDTH) ** -0.5),
        'norm_ffn_g': 1.0 + nrm(ks[15], (DEPTH, D_MODEL), 0.05),
        'w_up': nrm(ks[16], (DEPTH, D_MODEL, 2 * FFN_DIM), D_MODEL ** -0.5),
        'conv_ffn_w': nrm(ks[17], (DEPTH, FFN_CONV, 2 * FFN_DIM), FFN_CONV ** -0.5),
        'conv_ffn_b': nrm(ks[18], (DEPTH, 2 * FFN_DIM), 0.01),
        'w_down': nrm(ks[19], (DEPTH, FFN_DIM, D_MODEL), FFN_DIM ** -0.5),
        'final_norm_g': 1.0 + nrm(ks[20], (D_MODEL,), 0.05),
    }

def first_block(x, c, w_ada, b_ada, norm_mix_g, w_in, rel_bias, attn_norm_g, conv_ssm_w, conv_ssm_b,
              dt_bias, a_log, d_skip, ssm_norm_g, w_out, norm_ffn_g, w_up, conv_ffn_w, conv_ffn_b,
              w_down, final_norm_g):
    bsz, s, _ = x.shape
    gn = N_SSM_GROUPS * D_STATE
    sizes = [ATTN_WIDTH, ATTN_WIDTH, ATTN_WIDTH, SSM_WIDTH, SSM_WIDTH, gn, gn, N_SSM_HEADS]
    split_at = [int(v) for v in np.cumsum(sizes)[:-1]]
    for l in range(DEPTH):
        mod = jax.nn.silu(c) @ w_ada[l] + b_ada[l]
        shift_m, scale_m, gate_m, shift_f, scale_f, gate_f = jnp.split(mod[:, None, :], 6, axis=-1)
        h = rms_norm(x, norm_mix_g[l]) * (1.0 + scale_m) + shift_m
        proj = h @ w_in[l]
        q, k, v, xs, z, bmat, cmat, dt_raw = jnp.split(proj, split_at, axis=-1)
        hd = (bsz, s, N_ATTN_HEADS, ATTN_HEAD_DIM)
        attn = moba_attention(q.reshape(hd), k.reshape(hd), v.reshape(hd), rel_bias)
        attn = rms_norm(attn, attn_norm_g[l])
        ssm = ssd_mixer(xs, z, bmat, cmat, dt_raw, conv_ssm_w[l], conv_ssm_b[l], dt_bias[l],
                        a_log[l], d_skip[l], ssm_norm_g[l])
        mix = jnp.concatenate([attn, ssm], axis=-1) @ w_out[l]
        x = x + gate_m * mix
        h = rms_norm(x, norm_ffn_g[l]) * (1.0 + scale_f) + shift_f
        x = x + gate_f * conv_ffn(h, w_up[l], conv_ffn_w[l], conv_ffn_b[l], w_down[l])
    return rms_norm(x, final_norm_g)


GRID_W = 64
MEM_LEN = 256

NA_HEADS = 8
NA_HEAD_DIM = 128
NA_WIDTH = NA_HEADS * NA_HEAD_DIM
NA_ROWS_MAX = 8
NA_COLS = 16

MLA_HEADS = 8
MLA_Q_RANK = 512
MLA_KV_RANK = 256
MLA_NOPE_DIM = 128
MLA_ROPE_DIM = 64
MLA_V_DIM = 128
MLA_QK_DIM = MLA_NOPE_DIM + MLA_ROPE_DIM
MLA_WIDTH = MLA_HEADS * MLA_V_DIM
ROPE_THETA = 10000.0
Q_BLOCK = 128

D_MIX = NA_WIDTH + MLA_WIDTH
IN_WIDTH = 3 * NA_WIDTH + MLA_Q_RANK + MLA_KV_RANK + MLA_ROPE_DIM

X_HEADS = 4
X_HEAD_DIM = D_MODEL // X_HEADS

D_FF = ((8 * D_MODEL + 3 * 256 - 1) // (3 * 256)) * 256


def rmsnorm(x, g):
    xf = x.astype(jnp.float32)
    y = xf * lax.rsqrt(jnp.mean(xf * xf, axis=-1, keepdims=True) + EPS)
    return (y * g.astype(jnp.float32)).astype(x.dtype)

def rope_tables(seq_len):
    inv = 1.0 / (ROPE_THETA ** (jnp.arange(0, MLA_ROPE_DIM, 2, dtype=jnp.float32) / MLA_ROPE_DIM))
    ang = jnp.arange(seq_len, dtype=jnp.float32)[:, None] * inv[None, :]
    return jnp.cos(ang), jnp.sin(ang)

def apply_rope(x, cos, sin):
    xf = x.astype(jnp.float32)
    x1, x2 = jnp.split(xf, 2, axis=-1)
    return jnp.concatenate([x1 * cos - x2 * sin, x1 * sin + x2 * cos], axis=-1).astype(x.dtype)

def neighbourhood_attention(q, k, v, rpb):
    B, S, H, dh = q.shape
    rows = S // GRID_W
    kr = min(NA_ROWS_MAX, rows)
    qg = q.reshape(B, rows, GRID_W, H, dh)
    kg = k.reshape(B, rows, GRID_W, H, dh)
    vg = v.reshape(B, rows, GRID_W, H, dh)
    row_start = jnp.clip(jnp.arange(rows) - kr // 2, 0, rows - kr)
    col_start = np.clip(np.arange(GRID_W) - NA_COLS // 2, 0, GRID_W - NA_COLS)
    col_idx = col_start[:, None] + np.arange(NA_COLS)[None, :]
    dc = col_idx - np.arange(GRID_W)[:, None] + (NA_COLS - 1)
    bias_c = rpb[:, :, dc]
    scale = dh ** -0.5

    def one_row(r):
        rs = row_start[r]
        kb = lax.dynamic_slice_in_dim(kg, rs, kr, axis=1)[:, :, col_idx]
        vb = lax.dynamic_slice_in_dim(vg, rs, kr, axis=1)[:, :, col_idx]
        qr = lax.dynamic_index_in_dim(qg, r, axis=1, keepdims=False)
        s = jnp.einsum('bqhd,brqkhd->bhqrk', qr, kb).astype(jnp.float32) * scale
        dr = rs + jnp.arange(kr) - r + (NA_ROWS_MAX - 1)
        bias = jnp.transpose(bias_c[:, dr], (0, 2, 1, 3)).astype(jnp.float32)
        s = s + bias[None]
        p = jax.nn.softmax(s.reshape(B, H, GRID_W, kr * NA_COLS), axis=-1)
        p = p.reshape(B, H, GRID_W, kr, NA_COLS).astype(v.dtype)
        return jnp.einsum('bhqrk,brqkhd->bqhd', p, vb)

    out = lax.map(one_row, jnp.arange(rows))
    return jnp.moveaxis(out, 0, 1).reshape(B, S, H * dh)

def latent_attention(c_q, c_kv, k_rope, q_norm, kv_norm, w_uq, w_ukv, cos, sin):
    B, S, _ = c_q.shape
    q = (rmsnorm(c_q, q_norm) @ w_uq).reshape(B, S, MLA_HEADS, MLA_QK_DIM)
    q_nope, q_rope = q[..., :MLA_NOPE_DIM], q[..., MLA_NOPE_DIM:]
    q_rope = apply_rope(q_rope, cos[:, None, :], sin[:, None, :])
    kv = (rmsnorm(c_kv, kv_norm) @ w_ukv).reshape(B, S, MLA_HEADS, MLA_NOPE_DIM + MLA_V_DIM)
    k_nope, v = kv[..., :MLA_NOPE_DIM], kv[..., MLA_NOPE_DIM:]
    k_r = apply_rope(k_rope, cos, sin)
    nb = S // Q_BLOCK
    qn_b = jnp.moveaxis(q_nope.reshape(B, nb, Q_BLOCK, MLA_HEADS, MLA_NOPE_DIM), 1, 0)
    qr_b = jnp.moveaxis(q_rope.reshape(B, nb, Q_BLOCK, MLA_HEADS, MLA_ROPE_DIM), 1, 0)
    scale = MLA_QK_DIM ** -0.5

    def block(args):
        qn, qr = args
        s = (jnp.einsum('bqhd,bkhd->bhqk', qn, k_nope)
             + jnp.einsum('bqhr,bkr->bhqk', qr, k_r)).astype(jnp.float32) * scale
        p = jax.nn.softmax(s, axis=-1).astype(v.dtype)
        return jnp.einsum('bhqk,bkhd->bqhd', p, v)

    out = lax.map(block, (qn_b, qr_b))
    return jnp.moveaxis(out, 0, 1).reshape(B, S, MLA_WIDTH)

def memory_attention(h, mem_n, w_q, w_k, w_v, w_o):
    B, S, _ = h.shape
    M = mem_n.shape[1]
    q = (h @ w_q).reshape(B, S, X_HEADS, X_HEAD_DIM)
    k = (mem_n @ w_k).reshape(B, M, X_HEADS, X_HEAD_DIM)
    v = (mem_n @ w_v).reshape(B, M, X_HEADS, X_HEAD_DIM)
    s = jnp.einsum('bqhd,bkhd->bhqk', q, k).astype(jnp.float32) * (X_HEAD_DIM ** -0.5)
    p = jax.nn.softmax(s, axis=-1).astype(v.dtype)
    o = jnp.einsum('bhqk,bkhd->bqhd', p, v).reshape(B, S, D_MODEL)
    return o @ w_o

def swiglu(h, w_gate, w_up, w_down):
    return (jax.nn.silu(h @ w_gate) * (h @ w_up)) @ w_down

def second_inputs(seed: int = 0) -> dict:
    key = jax.random.key(seed)
    ks = jax.random.split(key, 24)

    def dense(k, shape, fan_in):
        return jax.random.normal(k, shape, jnp.float32) * (fan_in ** -0.5)

    def gain(k, shape):
        return 1.0 + 0.02 * jax.random.normal(k, shape, jnp.float32)

    L = DEPTH
    return {
        "x": jax.random.normal(ks[0], (BATCH, SEQ, D_MODEL), jnp.float32),
        "mem": jax.random.normal(ks[1], (BATCH, MEM_LEN, D_MODEL), jnp.float32),
        "ln_mix": gain(ks[2], (L, D_MODEL)),
        "w_in": dense(ks[3], (L, D_MODEL, IN_WIDTH), D_MODEL),
        "q_norm": gain(ks[4], (L, MLA_Q_RANK)),
        "kv_norm": gain(ks[5], (L, MLA_KV_RANK)),
        "w_uq": dense(ks[6], (L, MLA_Q_RANK, MLA_HEADS * MLA_QK_DIM), MLA_Q_RANK),
        "w_ukv": dense(ks[7], (L, MLA_KV_RANK, MLA_HEADS * (MLA_NOPE_DIM + MLA_V_DIM)), MLA_KV_RANK),
        "na_rpb": 0.1 * jax.random.normal(ks[8], (L, NA_HEADS, 2 * NA_ROWS_MAX - 1, 2 * NA_COLS - 1), jnp.float32),
        "na_out_norm": gain(ks[9], (L, NA_WIDTH)),
        "mla_out_norm": gain(ks[10], (L, MLA_WIDTH)),
        "w_out": dense(ks[11], (L, D_MIX, D_MODEL), D_MIX),
        "ln_mem": gain(ks[12], (L, D_MODEL)),
        "mem_norm": gain(ks[13], (L, D_MODEL)),
        "w_xq": dense(ks[14], (L, D_MODEL, D_MODEL), D_MODEL),
        "w_xk": dense(ks[15], (L, D_MODEL, D_MODEL), D_MODEL),
        "w_xv": dense(ks[16], (L, D_MODEL, D_MODEL), D_MODEL),
        "w_xo": dense(ks[17], (L, D_MODEL, D_MODEL), D_MODEL),
        "ln_ffn": gain(ks[18], (L, D_MODEL)),
        "w_gate": dense(ks[19], (L, D_MODEL, D_FF), D_MODEL),
        "w_up": dense(ks[20], (L, D_MODEL, D_FF), D_MODEL),
        "w_down": dense(ks[21], (L, D_FF, D_MODEL), D_FF),
        "final_norm": gain(ks[22], (D_MODEL,)),
    }

def second_block(x, mem, ln_mix, w_in, q_norm, kv_norm, w_uq, w_ukv, na_rpb, na_out_norm,
              mla_out_norm, w_out, ln_mem, mem_norm, w_xq, w_xk, w_xv, w_xo, ln_ffn,
              w_gate, w_up, w_down, final_norm):
    B, S, _ = x.shape
    cos, sin = rope_tables(S)
    o1 = NA_WIDTH
    o2 = 2 * NA_WIDTH
    o3 = 3 * NA_WIDTH
    o4 = o3 + MLA_Q_RANK
    o5 = o4 + MLA_KV_RANK
    for l in range(DEPTH):
        h = rmsnorm(x, ln_mix[l])
        proj = h @ w_in[l]
        q_na = proj[..., :o1].reshape(B, S, NA_HEADS, NA_HEAD_DIM)
        k_na = proj[..., o1:o2].reshape(B, S, NA_HEADS, NA_HEAD_DIM)
        v_na = proj[..., o2:o3].reshape(B, S, NA_HEADS, NA_HEAD_DIM)
        c_q = proj[..., o3:o4]
        c_kv = proj[..., o4:o5]
        k_rope = proj[..., o5:]
        y_na = neighbourhood_attention(q_na, k_na, v_na, na_rpb[l])
        y_mla = latent_attention(c_q, c_kv, k_rope, q_norm[l], kv_norm[l], w_uq[l], w_ukv[l], cos, sin)
        y = jnp.concatenate([rmsnorm(y_na, na_out_norm[l]), rmsnorm(y_mla, mla_out_norm[l])], axis=-1)
        x = x + y @ w_out[l]
        h = rmsnorm(x, ln_mem[l])
        x = x + memory_attention(h, rmsnorm(mem, mem_norm[l]), w_xq[l], w_xk[l], w_xv[l], w_xo[l])
        h = rmsnorm(x, ln_ffn[l])
        x = x + swiglu(h, w_gate[l], w_up[l], w_down[l])
    return rmsnorm(x, final_norm)


def setup_inputs(seed=0):
    out = dict(first_inputs(seed))
    for name, value in second_inputs(seed + 1).items():
        if name != "x":
            out[name + "_2"] = value
    return out


def reference(
    x, c, w_ada, b_ada, norm_mix_g, w_in, rel_bias, attn_norm_g, conv_ssm_w, conv_ssm_b,
    dt_bias, a_log, d_skip, ssm_norm_g, w_out, norm_ffn_g, w_up, conv_ffn_w, conv_ffn_b, w_down,
    final_norm_g, mem_2, ln_mix_2, w_in_2, q_norm_2, kv_norm_2, w_uq_2, w_ukv_2, na_rpb_2,
    na_out_norm_2, mla_out_norm_2, w_out_2, ln_mem_2, mem_norm_2, w_xq_2, w_xk_2, w_xv_2,
    w_xo_2, ln_ffn_2, w_gate_2, w_up_2, w_down_2, final_norm_2,
):
    x = first_block(
        x, c, w_ada, b_ada, norm_mix_g, w_in, rel_bias, attn_norm_g, conv_ssm_w, conv_ssm_b,
        dt_bias, a_log, d_skip, ssm_norm_g, w_out, norm_ffn_g, w_up, conv_ffn_w, conv_ffn_b,
        w_down, final_norm_g,
    )
    return second_block(
        x, mem_2, ln_mix_2, w_in_2, q_norm_2, kv_norm_2, w_uq_2, w_ukv_2, na_rpb_2,
        na_out_norm_2, mla_out_norm_2, w_out_2, ln_mem_2, mem_norm_2, w_xq_2, w_xk_2, w_xv_2,
        w_xo_2, ln_ffn_2, w_gate_2, w_up_2, w_down_2, final_norm_2,
    )


_drawn_inputs = setup_inputs


def setup_inputs(seed=0):
    import zlib

    import numpy as np

    out = dict(_drawn_inputs(seed))
    spreads = {}
    factors = {'norm_mix_g': 2.761,
     'conv_ssm_b': 8.0,
     'd_skip': 4.111,
     'ssm_norm_g': 3.47,
     'norm_ffn_g': 3.278,
     'conv_ffn_b': 8.0,
     'ln_mix_2': 2.926,
     'q_norm_2': 8.0,
     'kv_norm_2': 4.916,
     'na_out_norm_2': 5.122,
     'mla_out_norm_2': 5.479,
     'ln_mem_2': 8.0,
     'mem_norm_2': 8.0,
     'ln_ffn_2': 5.037,
     'final_norm_2': 2.789}
    for name, (base, spread) in spreads.items():
        noise = np.random.default_rng([zlib.crc32(name.encode()), seed]).standard_normal(out[name].shape)
        drawn = base * np.exp(spread * noise) if base else spread * noise
        out[name] = __import__('jax').numpy.asarray(drawn.astype(out[name].dtype))
    for name, factor in factors.items():
        out[name] = (out[name] * factor).astype(out[name].dtype)
    return out
```

```python
from contextlib import ExitStack

import numpy as np
import concourse.bass as bass
from concourse import mybir

F32 = mybir.dt.float32
F32R = mybir.dt.float32r
I32 = mybir.dt.int32
ALU = mybir.AluOpType
ACT = mybir.ActivationFunctionType
AX_X = mybir.AxisListType.X

P = 128
D = 2048
S = 256
FF = 5632
FC = FF // P
EPS = 1e-6
MASKED = -3.0e38
TILE = 2048
HALF = TILE // 2
RAW = 4
SLOTS = 4
HD = 128
NH = 8
XH = 4
STATE_HEADS = 16
REL = 512
NA_W = 127
GRID = 64

STREAM = [("xk", 16), ("xv", 16), ("win", 44), ("dt", 1), ("wout", 16), ("up", 88), ("down", 44),
          ("win2", 32), ("uq", 3), ("ukv", 2), ("wout2", 16), ("xq", 16), ("xo", 16), ("gu", 88),
          ("down2", 44)]
T0, _t = {}, 0
for _name, _n in STREAM:
    T0[_name] = _t
    _t += _n
TILES = _t
H0 = {k: 2 * v for k, v in T0.items()}

GROUPS = [("xk", 4), ("xv", 4), ("win", 11), ("dt", 1), ("wout", 4), ("up", 22), ("down", 2),
          ("win2", 8), ("uq", 3), ("ukv", 4), ("wout2", 4), ("xq", 4), ("xo", 4), ("gu", 22),
          ("down2", 2)]
G0, _g = {}, 0
for _name, _n in GROUPS:
    G0[_name] = _g
    _g += _n

ADA_ORDER = [1, 0, 2, 4, 3, 5]
ADA_UNITS = 4 * len(ADA_ORDER)

VEC = [("c", 16), ("b_ada", 96), ("mix_g", 16), ("attn_g", 8), ("ssm_g", 8), ("cs_w", 48),
       ("cs_b", 12), ("dskip", 8), ("ffn_g", 16), ("cf_b", 88), ("cf_w", 264),
       ("fin_g", 16), ("lnmix_g", 16), ("q_g", 4), ("kv_g", 2), ("na_g", 8), ("mla_g", 8),
       ("lnmem_g", 16), ("mem_g", 16), ("lnffn_g", 16), ("fin2_g", 16), ("dtb", 16), ("alog", 16)]
V0, _v = {}, 0
for _name, _n in VEC:
    V0[_name] = _v
    _v += _n
NVEC = _v

CONST = [("tri", 256), ("after", 128), ("ident", 128), ("cos", 256), ("sin", 256), ("rot", 128),
         ("window", 64)]
C0, _c = {}, 0
for _name, _n in CONST:
    C0[_name] = _c
    _c += _n
NCONST = _c

NORMS = [("mem", [(16, D)]), ("mix", [(16, D)]), ("mixin", [(8, 1024), (4, 512), (4, 512)]),
         ("ffn", [(16, D)]), ("fin", [(16, D)]), ("lnmix", [(16, D)]), ("qkv", [(4, 512), (2, 256)]),
         ("mixin2", [(8, 1024), (8, 1024)]), ("lnmem", [(16, D)]), ("lnffn", [(16, D)]),
         ("fin2", [(16, D)])]


def quads_of(groups):
    out, c = [], 0
    for g, (n, _) in enumerate(groups):
        for a in range(0, n, 4):
            out.append((g, c + a, min(4, n - a), a == 0, a + 4 >= n))
        c += n
    return out


SQ0, AL0, _q, _a = {}, {}, 0, 0
for _name, _groups in NORMS:
    SQ0[_name] = _q
    AL0[_name] = _a
    _q += len(quads_of(_groups))
    if _name not in ("fin", "fin2"):
        _a += len(quads_of(_groups))
NORM_AT = {n: i for i, (n, _) in enumerate(NORMS)}
NORM_GROUPS = dict(NORMS)
AL_XO = _a


def al_before(name):
    if name == "xo":
        return AL0["lnffn"]
    return AL0[name] + (4 if name == "lnffn" else 0)


def tmp_at(first):
    return first if first < al_before("lnffn") else first - 4


HEADS = {"moba": 0, "na": 8, "mla": 16, "x": 24}


def block_program(nc, stream, ada, xT, memT, vecs, consts, onehot, relb, rpb, out, rel_dram,
                  rpb_dram, k_dram, v_dram):
    ctx = ExitStack()
    with ctx:
        def sb(name, shape, dt=F32):
            return ctx.enter_context(nc.sbuf_tensor(name, shape, dt))

        def sem(name):
            return ctx.enter_context(nc.semaphore(name))

        raw = sb("raw", [P, RAW, TILE])
        w_hi = sb("w_hi", [P, SLOTS, HALF], F32R)
        w_lo = sb("w_lo", [P, SLOTS, HALF], F32R)
        res = sb("res", [P, 16, S])
        a_hi = sb("a_hi", [P, 16, S], F32R)
        a_lo = sb("a_lo", [P, 16, S], F32R)
        arena = sb("arena", [P, 15 * 1024])
        work = sb("work", [P, 4096])
        rstd = sb("rstd", [P, 3 * S])
        vec = sb("vec", [P, NVEC])
        con = sb("con", [P, NCONST])
        ones = sb("ones", [P, P])
        mod = sb("mod", [P, 6, 16])
        small = sb("small", [P, 64])
        dts = sb("dts", [P, 12, 32])

        def region(r, chunks=8, at=0):
            a = r * 2048 + at * S
            return arena[:, a:a + chunks * S].rearrange("p (c t) -> p c t", t=S)

        hidden = arena[:, 0:FC * S].rearrange("p (c t) -> p c t", t=S)
        ada_acc = arena[:, 11264:13312]
        ada_ring = arena[:, 13312:15360].rearrange("p (s n) -> p s n", s=2)
        q_r, k_r = region(0), region(1)
        v_r = arena[:, 4096:6144].rearrange("p (t n) -> p t n", t=2)
        xs_r, z_r, bc_r = region(3), region(4), region(5, 4)
        xtok = arena[:, 2048:4096].rearrange("p (t n) -> p t n", t=2)
        ckv_r, qn_r, kn_r = region(3), region(4), region(5)
        v2_r = arena[:, 12288:14336].rearrange("p (t n) -> p t n", t=2)
        qx_r, kx_r = region(0, 16), region(2, 16)
        vx_r = arena[:, 8192:12288].rearrange("p (t n) -> p t n", t=2)

        sq = work[:, 0:2048].rearrange("p (r n) -> p r n", r=2)
        tmp = work[:, 2048:4096].rearrange("p (r n) -> p r n", r=2)
        bias = work[:, 0:1024].rearrange("p (r n) -> p r n", r=2)
        logit = work[:, 1024:2048].rearrange("p (r n) -> p r n", r=2)
        prob = work[:, 2048:3072].rearrange("p (r n) -> p r n", r=2)
        probT = work[:, 3072:4096].rearrange("p (r n) -> p r n", r=2)
        conv = work[:, 0:2048].rearrange("p (r c t) -> p r c t", r=2, t=S)
        decay = work[:, 0:768].rearrange("p (r n) -> p r n", r=2)
        mix_m = work[:, 768:1536].rearrange("p (r n) -> p r n", r=2)
        seg_in = work[:, 1536:2304].rearrange("p (r n) -> p r n", r=2)
        gram = work[:, 2304:3072].rearrange("p (g n) -> p g n", g=2)

        ps = ctx.enter_context(nc.psum_tensor("ps", [P, 8, 512], F32))

        s_const, s_vec, s_res, s_mem = sem("s_const"), sem("s_vec"), sem("s_res"), sem("s_mem")
        raw_landed = [sem(f"raw_landed{i}") for i in range(RAW)]
        ada_landed = [sem(f"ada_landed{i}") for i in range(2)]
        hi_ready, lo_ready = sem("hi_ready"), sem("lo_ready")
        half_used = sem("half_used")
        evac = [sem("evac0"), sem("evac1")]
        evac_b = sem("evac_b")
        ones_ready = sem("ones_ready")
        ada_used, ada_summed, mod_ready = sem("ada_used"), sem("ada_summed"), sem("mod_ready")
        dve_step = sem("dve_step")
        sq_ready, sq_used, sum_done = sem("sq_ready"), sem("sq_used"), sem("sum_done")
        tmp_ready, ah_ready, al_ready = sem("tmp_ready"), sem("ah_ready"), sem("al_ready")
        res_ready = sem("res_ready")
        hid_ready, hs_ready, hl_ready = sem("hid_ready"), sem("hs_ready"), sem("hl_ready")
        silu_ready = sem("silu_ready")
        scr_stored, rel_landed = sem("scr_stored"), sem("rel_landed")
        rel_ps, rel_row = sem("rel_ps"), sem("rel_row")
        rpb_zero, rpb_in = sem("rpb_zero"), sem("rpb_in")
        bias_landed = [sem("bias_landed0"), sem("bias_landed1")]
        spill = [sem("spill0"), sem("spill1")]
        reload_done = sem("reload_done")
        s_ready, max_ready, exp_done, p_ready = (sem("s_ready"), sem("max_ready"),
                                                 sem("exp_done"), sem("p_ready"))
        pt_ready, pt_copied, o_ready, o_evac = (sem("pt_ready"), sem("pt_copied"),
                                                sem("o_ready"), sem("o_evac"))
        c_ready = sem("c_ready")
        dt_exp, dt_done = sem("dt_exp"), sem("dt_done")
        xt_ready, xt_copied, gram_ready, gram_masked = (sem("xt_ready"), sem("xt_copied"),
                                                        sem("gram_ready"), sem("gram_masked"))
        seg_ready, seg_summed, decay_ready, m_ready, y_ready, y_done = (
            sem("seg_ready"), sem("seg_summed"), sem("decay_ready"), sem("m_ready"),
            sem("y_ready"), sem("y_done"))
        rot_ready, rot_done = sem("rot_ready"), sem("rot_done")
        out_ready, s_out = sem("out_ready"), sem("s_out")

        def col(name, i=0, n=1):
            return vec[:, V0[name] + i:V0[name] + i + n]

        def const(name, a=0, b=None):
            width = dict(CONST)[name]
            return con[:, C0[name] + a:C0[name] + (width if b is None else b)]

        def acc(G):
            return ps[:, 2 * (G % 2):2 * (G % 2) + 2, :].rearrange("p b (c t) -> p (b c) t", t=S)

        def acc_tok(G):
            return ps[:, 2 * (G % 2):2 * (G % 2) + 2, :]

        def acc_b(c):
            return ps[:, 4 + 2 * c:6 + 2 * c, :].rearrange("p b (c t) -> p (b c) t", t=S)

        block = ctx.enter_context(nc.Block())

        @block.sync
        def _(sp):
            def stream_tile(t, slot, first=False):
                if not first:
                    sp.wait_ge(lo_ready, t * 2 - 2 * RAW + 2)
                sp.dma_start(raw[:, slot], stream[t]).then_inc(raw_landed[slot], 16)

            def ada_unit(u, first=False):
                for i in range(8):
                    if not (first and i < 2):
                        sp.wait_ge(ada_used, u * 8 + (i - 1))
                    sp.dma_start(ada_ring[:, i % 2], ada[u * 8 + i]).then_inc(ada_landed[i % 2], 16)

            sp.dma_start(res[:, :, :], xT).then_inc(s_res, 16)
            sp.dma_start(vec[:, :], vecs).then_inc(s_vec, 16)
            sp.dma_start(region(0, 16), memT).then_inc(s_mem, 16)
            for t in range(4):
                stream_tile(t, t, True)
            ada_unit(0, True)
            with sp.Fori(1, 19) as g:
                for s in range(4):
                    stream_tile(g * 4 + s, s)
                ada_unit(g)
            stream_tile(76, 0)
            ada_unit(19)
            with sp.Fori(0, 4) as g:
                for s in range(4):
                    stream_tile(g * 4 + (77 + s), (77 + s) % 4)
                ada_unit(g + 20)
            turns = (TILES - 93) // 4
            with sp.Fori(0, turns) as g:
                for s in range(4):
                    stream_tile(g * 4 + (93 + s), (93 + s) % 4)
            for t in range(93 + 4 * turns, TILES):
                stream_tile(t, t % 4)
            for q in range(4):
                sp.wait_ge(out_ready, q + 1)
                sp.dma_start(out[:, 4 * q:4 * q + 4, :], res[:, 4 * q:4 * q + 4, :]).then_inc(s_out, 16)
            sp.wait_ge(s_out, 64)

        @block.gpsimd
        def _(pool):
            pool.memset(ones[:, :], 1.0).then_inc(ones_ready, 1)

            def low_part(h, slot, tile_slot, part):
                pool.wait_ge(hi_ready, h + 1)
                pool.tensor_tensor(w_lo[:, slot], raw[:, tile_slot, part * HALF:(part + 1) * HALF],
                                   w_hi[:, slot].bitcast(F32), ALU.subtract).then_inc(lo_ready, 1)

            with pool.Fori(0, TILES // 4) as i:
                for s in range(8):
                    low_part(i * 8 + s, s % 4, s // 2, s % 2)
            for t in range(TILES // 4 * 4, TILES):
                for part in range(2):
                    low_part(2 * t + part, (2 * t + part) % 4, t % 4, part)

        @block.scalar
        def _(act):
            def hi(h, base):
                n = base if h is None else h + base
                tile_slot = (base // 2) % 4
                count = 16 * (base // 8 + 1)
                act.wait_ge(raw_landed[tile_slot], count if h is None else h * 2 + count)
                if h is not None or base >= SLOTS:
                    act.wait_ge(half_used, n - SLOTS + 1)
                act.copy(w_hi[:, base % 4],
                         raw[:, tile_slot, (base % 2) * HALF:(base % 2 + 1) * HALF]).then_inc(hi_ready, 1)

            def his(base, n, h=None):
                for i in range(n):
                    hi(h, base + i)

            def squares(name, source, ready):
                for q, (_, c, n, _, _) in enumerate(quads_of(NORM_GROUPS[name])):
                    ready(q)
                    k = SQ0[name] + q
                    if k >= 2:
                        act.wait_ge(sq_used, k - 1)
                    act.activation(sq[:, k % 2, 0:n * S].rearrange("p (c t) -> p c t", t=S), source(c, n),
                                   ACT.Square).then_inc(sq_ready, 1)

            def split_high(first, chunks, halves_before, source=None):
                if halves_before:
                    act.wait_ge(half_used, halves_before)
                for q, (c, n) in enumerate(chunks):
                    k = first + q
                    if source is None:
                        act.wait_ge(tmp_ready, tmp_at(first) + q + 1)
                        src = tmp[:, (tmp_at(first) + q) % 2, 0:n * S].rearrange("p (c t) -> p c t", t=S)
                    else:
                        src = source(c, n)
                    act.copy(a_hi[:, c:c + n, :], src).then_inc(ah_ready, 1)

            def norm(name, source, ready, halves_before):
                squares(name, source, ready)
                if name not in ("fin", "fin2"):
                    split_high(al_before(name), [(c, n) for _, c, n, _, _ in quads_of(NORM_GROUPS[name])],
                               halves_before)

            def evac_copy(G, dst):
                act.copy(dst, acc(G)).then_inc(evac[G % 2], 1)

            def group_done(halves):
                act.wait_ge(half_used, halves)

            act.dma_start(con[:, :], consts).then_inc(s_const, 16)
            act.dma_start(work[0:32, 2048:2560], onehot).then_inc(rel_landed, 16)
            act.dma_start(work[0:32, 2560:2568], relb).then_inc(rel_landed, 16)
            act.wait_ge(rpb_zero, 1)
            act.dma_start(work[0:56, 3328 + 48:3328 + 79], rpb).then_inc(rpb_in, 16)

            act.wait_ge(s_vec, 16)
            act.activation(small[:, 16:32], col("c", 0, 16), ACT.Silu).then_inc(c_ready, 1)

            his(0, 4)
            act.wait_ge(s_mem, 16)
            squares("mem", lambda c, n: region(0, 16)[:, c:c + n, :], lambda q: None)
            act.wait_ge(rel_row, 1)
            act.dma_start(rel_dram, work[0:8, 2568:2568 + REL].unsqueeze(1).broadcast_to([8, P, REL])).then_inc(scr_stored, 16)
            act.wait_ge(rpb_in, 16)
            act.dma_start(rpb_dram, work[0:56, 3328:3328 + NA_W].unsqueeze(1).broadcast_to([56, GRID, NA_W])).then_inc(scr_stored, 16)
            split_high(0, [(c, n) for _, c, n, _, _ in quads_of(NORM_GROUPS["mem"])], 0)
            his(4, 4)

            stage = [arena[:, 4096:5120], arena[:, 5120:6144]]

            def spill_group(G, dst):
                if G >= 2:
                    act.wait_ge(spill[G % 2], 16 * (G // 2))
                act.copy(stage[G % 2], acc_tok(G).rearrange("p b n -> p (b n)")).then_inc(evac[G % 2], 1)
                act.wait_ge(evac[G % 2], G // 2 + 1)
                act.dma_start(dst, stage[G % 2]).then_inc(spill[G % 2], 16)

            for G in range(1, 8):
                his(8 * G, 4)
                group_done(8 * G)
                spill_group(G - 1, k_dram[G - 1] if G - 1 < 4 else v_dram[G - 5])
                his(8 * G + 4, 4)

            his(H0["win"], 4)
            group_done(H0["win"])
            spill_group(7, v_dram[3])
            act.wait_ge(s_res, 16)
            norm("mix", lambda c, n: res[:, c:c + n, :], lambda q: None, H0["win"])
            his(H0["win"] + 4, 4)
            act.wait_ge(spill[0], 64)
            act.wait_ge(spill[1], 64)
            for g in range(1, 12):
                last = g == 11
                his(H0["win"] + 8 * g, 2 if last else 4)
                group_done(H0["win"] + 8 * g)
                G = G0["win"] + g - 1
                if g - 1 < 4:
                    if g == 1:
                        act.wait_ge(tmp_ready, 4)
                    evac_copy(G, region(0, 16)[:, 4 * (g - 1):4 * g, :])
                elif g - 1 < 6:
                    j = g - 1 - 4
                    act.copy(v_r[:, :, 512 * j:512 * j + 512], acc_tok(G)).then_inc(evac[G % 2], 1)
                elif g - 1 in (6, 7):
                    j = g - 1 - 6
                    act.wait_ge(evac[G % 2], G // 2 + 1)
                    act.activation(xs_r[:, 4 * j:4 * j + 4, :], conv[:, j % 2], ACT.Silu).then_inc(silu_ready, 1)
                elif g - 1 in (8, 9):
                    j = g - 1 - 8
                    act.activation(z_r[:, 4 * j:4 * j + 4, :], acc(G), ACT.Silu).then_inc(evac[G % 2], 1)
                else:
                    act.wait_ge(evac[G % 2], G // 2 + 1)
                    act.activation(bc_r[:, :, :], conv[:, 0], ACT.Silu).then_inc(silu_ready, 1)
                if not last:
                    his(H0["win"] + 8 * g + 4, 4)
            his(H0["wout"], 2)

            def load_bias(u, kind, h):
                slot = bias[:, u % 2, :]
                if kind == "moba":
                    for qt in range(2):
                        src = bass.AP(rel_dram.tensor, h * P * REL + S - 1 - P * qt, [[REL - 1, P], [1, S]])
                        act.dma_start(slot[:, qt * S:(qt + 1) * S], src).then_inc(bias_landed[u % 2], 16)
                else:
                    for qt in range(2):
                        for a in range(2):
                            off = (7 * h + 3 - 2 * qt - a) * GRID * NA_W + GRID - 1
                            src = bass.AP(rpb_dram.tensor, off,
                                          [[NA_W - 1, GRID], [GRID * NA_W, 4], [1, GRID]])
                            dst = slot[a * GRID:(a + 1) * GRID, qt * S:(qt + 1) * S]
                            act.dma_start(dst.rearrange("p (r c) -> p r c", c=GRID), src)\
                               .then_inc(bias_landed[u % 2], 16)

            def attention(kind, dst, scale, chunks=1):
                u0 = HEADS[kind]
                n = XH if kind == "x" else NH
                biased = kind in ("moba", "na")

                def exp(u):
                    act.wait_ge(max_ready, u + 1)
                    src = logit[:, u % 2, :] if biased else ps[:, 4 + u % 2, :]
                    for qt in range(2):
                        ins = act.activation(prob[:, u % 2, qt * S:(qt + 1) * S], src[:, qt * S:(qt + 1) * S],
                                             ACT.Exp, bias=small[:, 4 * (u % 2) + qt:4 * (u % 2) + qt + 1],
                                             scale=1.0 if biased else scale,
                                             accum_out=small[:, 8 + 4 * (u % 2) + qt:9 + 4 * (u % 2) + qt])
                    ins.then_inc(exp_done, 1)
                    if biased and u + 2 < u0 + n:
                        load_bias(u + 2, kind, u + 2 - u0)

                def copies(u):
                    act.wait_ge(pt_ready, u + 1)
                    act.copy(probT[:, u % 2, :], ps[:, 6 + u % 2, :]).then_inc(pt_copied, 1)

                def output(u):
                    act.wait_ge(o_ready, u + 1)
                    h = u - u0
                    act.copy(dst[:, h * chunks:(h + 1) * chunks, :],
                             ps[:, 2 * (u % 2):2 * (u % 2) + 2, :].rearrange("p b (c t) -> p (b c) t", t=S)
                             [:, 0:chunks, :]).then_inc(o_evac, 1)

                exp(u0)
                for u in range(u0, u0 + n):
                    if u + 1 < u0 + n:
                        exp(u + 1)
                    copies(u)
                    if u > u0:
                        output(u - 1)
                output(u0 + n - 1)

            act.wait_ge(scr_stored, 32)
            act.wait_ge(silu_ready, 3)
            load_bias(0, "moba", 0)
            load_bias(1, "moba", 1)
            attention("moba", q_r, HD ** -0.5)

            act.wait_ge(dt_done, 1)
            act.activation(dts[:, 2, :], dts[:, 1, :], ACT.Exp)
            act.activation(dts[:, 3, 0:16], col("alog", 0, 16), ACT.Exp).then_inc(dt_exp, 1)
            for tt in range(2):
                for hf in range(2):
                    act.wait_ge(xt_ready, 2 * tt + hf + 1)
                    act.copy(xtok[:, tt, hf * 512:(hf + 1) * 512], ps[:, 2 * tt + hf, :]).then_inc(xt_copied, 1)
            for h in range(STATE_HEADS):
                act.wait_ge(seg_summed, h + 1)
                if h >= 2:
                    act.wait_ge(m_ready, h - 1)
                act.activation(decay[:, h % 2, :], ps[:, 6 + h % 2, 0:384], ACT.Exp).then_inc(decay_ready, 1)

            def mixin_ready(q):
                act.wait_ge(y_done, 8)

            def mixin_source(c, n):
                return q_r[:, c:c + n, :] if c < 8 else z_r[:, c - 8:c - 8 + n, :]

            def residual_ready(name):
                def wait(q):
                    if name == "fin":
                        act.wait_ge(res_ready, q + 1)
                    elif name in ("down", "down2") and q >= 2:
                        act.wait_ge(evac_b, 2 * (name == "down2") + q - 1)
                    else:
                        G = G0[name] + q
                        act.wait_ge(evac[G % 2], G // 2 + 1)
                return wait

            his(H0["wout"] + 2, 2)
            norm("mixin", mixin_source, mixin_ready, H0["wout"])
            his(H0["wout"] + 4, 4)
            his(H0["wout"] + 8, 24)
            his(H0["up"], 4)
            norm("ffn", lambda c, n: res[:, c:c + n, :], residual_ready("wout"), H0["up"])
            his(H0["up"] + 4, 4)

            def ffn_silu(par, G, i=None):
                act.wait_ge(evac[G % 2], G // 2 + 1 if i is None else i + (G // 2 + 1))
                act.activation(conv[:, par, 0:2, :], conv[:, par, 0:2, :], ACT.Silu).then_inc(silu_ready, 1)

            his(H0["up"] + 8, 4)
            ffn_silu(0, G0["up"])
            his(H0["up"] + 12, 4)
            with act.Fori(0, 10) as i:
                for p in range(2):
                    his(H0["up"] + 16 + 8 * p, 4, h=i * 16)
                    ffn_silu((1 + p) % 2, G0["up"] + 1 + p, i)
                    his(H0["up"] + 20 + 8 * p, 4, h=i * 16)
            his(H0["down"], 2)
            ffn_silu(1, G0["up"] + 21)
            his(H0["down"] + 2, 2)

            def hidden_high(n, quad, base_hs):
                act.copy(a_hi[:, (n % 2) * 4:(n % 2) * 4 + 4, :],
                         hidden[:, bass.ds(quad * 4, 4), :] if not isinstance(quad, int)
                         else hidden[:, 4 * quad:4 * quad + 4, :]).then_inc(hs_ready, 1)

            def down(name):
                base = H0[name]
                if name == "down":
                    act.wait_ge(hid_ready, 22)
                else:
                    for G in (G0["gu"] + 20, G0["gu"] + 21):
                        act.wait_ge(evac[G % 2], G // 2 + 1)
                act.wait_ge(half_used, base)
                hidden_high(0, 0, 0)
                hidden_high(1, 1, 0)
                his(base + 4, 4)
                for n in range(2, 22):
                    act.wait_ge(half_used, base + 4 * (n - 1))
                    hidden_high(n, n % 11, 0)
                    his(base + 4 * n, 4)

            down("down")

            his(H0["win2"], 4)
            norm("fin", lambda c, n: res[:, c:c + n, :], residual_ready("down"), 0)
            norm("lnmix", lambda c, n: res[:, c:c + n, :], residual_ready("fin"), H0["win2"])
            his(H0["win2"] + 4, 4)
            for g in range(1, 9):
                if g < 8:
                    his(H0["win2"] + 8 * g, 4)
                else:
                    his(H0["uq"], 2)
                group_done(H0["win2"] + 8 * g)
                G = G0["win2"] + g - 1
                if g - 1 < 4:
                    evac_copy(G, region(0, 16)[:, 4 * (g - 1):4 * g, :])
                elif g - 1 < 6:
                    j = g - 1 - 4
                    act.copy(v_r[:, :, 512 * j:512 * j + 512], acc_tok(G)).then_inc(evac[G % 2], 1)
                elif g - 1 == 6:
                    evac_copy(G, ckv_r[:, 0:4, :])
                else:
                    act.copy(ckv_r[:, 4:7, :], acc(G)[:, 0:3, :]).then_inc(evac[G % 2], 1)
                if g < 8:
                    his(H0["win2"] + 8 * g + 4, 4)

            def ckv_ready(q):
                G = G0["win2"] + 6 + q
                act.wait_ge(evac[G % 2], G // 2 + 1)

            norm("qkv", lambda c, n: ckv_r[:, c:c + n, :], ckv_ready, H0["uq"])
            his(H0["uq"] + 2, 2)
            lat = H0["uq"]
            dsts = [(2, qn_r[:, 0:4, :]), (4, qn_r[:, 4:8, :]), (6, ckv_r[:, 0:4, :]),
                    (7, kn_r[:, 0:4, :]), (8, kn_r[:, 4:8, :]), (9, 0), (10, 1)]
            issued = 4
            for i, (used, dst) in enumerate(dsts):
                want = min(used + 3, 14)
                if want > issued:
                    his(lat + issued, want - issued)
                    issued = want
                group_done(lat + used)
                G = G0["uq"] + i
                if isinstance(dst, int):
                    act.copy(v2_r[:, :, 512 * dst:512 * dst + 512], acc_tok(G)).then_inc(evac[G % 2], 1)
                else:
                    if i == 2:
                        act.wait_ge(tmp_ready, tmp_at(al_before("qkv")) + 2)
                    act.copy(dst, acc(G)).then_inc(evac[G % 2], 1)
            if issued < 14:
                his(lat + issued, 14 - issued)

            act.wait_ge(al_ready, al_before("qkv") + 2)
            load_bias(8, "na", 0)
            load_bias(9, "na", 1)
            attention("na", q_r, HD ** -0.5)
            attention("mla", qn_r, 192 ** -0.5)

            def mixin2_source(c, n):
                return q_r[:, c:c + n, :] if c < 8 else qn_r[:, c - 8:c - 8 + n, :]

            norm("mixin2", mixin2_source, lambda q: act.wait_ge(o_evac, 16 if q < 2 else 24), H0["wout2"])
            act.wait_ge(al_ready, al_before("mixin2") + 4)
            act.wait_ge(spill[0], 64)
            for j in range(4):
                act.dma_start(kx_r[:, 4 * j:4 * j + 4, :], k_dram[j].rearrange("p (c t) -> p c t", t=S))\
                   .then_inc(reload_done, 16)
                act.dma_start(vx_r[:, :, 512 * j:512 * j + 512], v_dram[j].rearrange("p (t n) -> p t n", t=2))\
                   .then_inc(reload_done, 16)
            his(H0["wout2"] + 4, 28)
            his(H0["xq"], 4)
            norm("lnmem", lambda c, n: res[:, c:c + n, :], residual_ready("wout2"), H0["xq"])
            his(H0["xq"] + 4, 4)
            for g in range(1, 5):
                if g < 4:
                    his(H0["xq"] + 8 * g, 4)
                else:
                    his(H0["xo"], 4)
                group_done(H0["xq"] + 8 * g)
                evac_copy(G0["xq"] + g - 1, qx_r[:, 4 * (g - 1):4 * g, :])
                if g < 4:
                    his(H0["xq"] + 8 * g + 4, 4)
            attention("x", qx_r, 512 ** -0.5, chunks=4)
            act.wait_ge(half_used, H0["xo"])
            for q in range(4):
                act.wait_ge(o_evac, 25 + q)
                act.copy(a_hi[:, 4 * q:4 * q + 4, :], qx_r[:, 4 * q:4 * q + 4, :]).then_inc(ah_ready, 1)
            his(H0["xo"] + 4, 28)
            his(H0["gu"], 4)
            norm("lnffn", lambda c, n: res[:, c:c + n, :], residual_ready("xo"), H0["gu"])
            his(H0["gu"] + 4, 4)

            def gate_silu(par, G_par, used, used_prev):
                act.wait_ge(half_used, used)
                if used_prev is not None:
                    act.wait_ge(evac[G_par % 2], used_prev)
                act.activation(conv[:, par, 0:2, :], acc(G_par)[:, 0:2, :], ACT.Silu).then_inc(silu_ready, 1)

            gb = H0["gu"]
            his(gb + 8, 4)
            gate_silu(0, G0["gu"], gb + 8, None)
            his(gb + 12, 4)
            with act.Fori(0, 10) as i:
                for p in range(2):
                    his(gb + 16 + 8 * p, 4, h=i * 16)
                    gate_silu((1 + p) % 2, G0["gu"] + 1 + p, i * 16 + (gb + 16 + 8 * p),
                              i + (G0["gu"] + 1 + p) // 2)
                    his(gb + 20 + 8 * p, 4, h=i * 16)
            his(H0["down2"], 2)
            gate_silu(1, G0["gu"] + 21, gb + 8 * 22, (G0["gu"] + 21) // 2)
            his(H0["down2"] + 2, 2)
            down("down2")
            norm("fin2", lambda c, n: res[:, c:c + n, :], residual_ready("down2"), 0)

        @block.tensor
        def _(pe):
            def wait_half(n):
                pe.wait_ge(hi_ready, n)
                pe.wait_ge(lo_ready, n)

            def half_T(slot, out4, c0, first, last, chunks=4, inc=True):
                for k in range(2):
                    for f in range(chunks):
                        w = slice(k * 512 + f * P, k * 512 + (f + 1) * P)
                        o = out4[:, f, :]
                        pe.matmul(o, w_hi[:, slot, w], a_hi[:, c0 + k, :], start=first and k == 0 and f % 2 == 0,
                                  stop=False, skip_group_check=True)
                        pe.matmul(o, w_hi[:, slot, w], a_lo[:, c0 + k, :], start=False, stop=False,
                                  skip_group_check=True)
                        mm = pe.matmul(o, w_lo[:, slot, w], a_hi[:, c0 + k, :], start=False,
                                       stop=last and k == 1, skip_group_check=True)
                mm.then_inc(half_used, 1)

            def half_N(slot, out2, c0, first, last, width=512):
                for k in range(2):
                    for t in range(2):
                        w = slice(k * 512, k * 512 + width)
                        a = slice(t * P, (t + 1) * P)
                        pe.matmul(out2[:, t, 0:width], a_hi[:, c0 + k, a], w_hi[:, slot, w],
                                  start=first and k == 0, stop=False, skip_group_check=True)
                        pe.matmul(out2[:, t, 0:width], a_lo[:, c0 + k, a], w_hi[:, slot, w],
                                  start=False, stop=False, skip_group_check=True)
                        mm = pe.matmul(out2[:, t, 0:width], a_hi[:, c0 + k, a], w_lo[:, slot, w],
                                       start=False, stop=last and k == 1, skip_group_check=True)
                mm.then_inc(half_used, 1)

            def al_quad(k):
                pe.wait_ge(al_ready, k)

            def group(kind, G, h0, al=None, i=None, chunks=4):
                n = G // 2
                pe.wait_ge(evac[G % 2], n if i is None else i + n) if (i is not None or n) else None
                for s in range(8):
                    wait_half(h0 + s + 1 if i is None else i * 16 + (h0 + s + 1))
                    if al is not None and s % 2 == 0:
                        al_quad(al + s // 2 + 1)
                    if kind == "T":
                        half_T((h0 + s) % 4, acc(G), 2 * s, s == 0, s == 7, chunks)
                    else:
                        half_N((h0 + s) % 4, acc_tok(G), 2 * s, s == 0, s == 7)

            def groups(kind, name, a, b, al=None):
                G, h = G0[name], H0[name]
                if al is not None:
                    group(kind, G + a, h + 8 * a, al)
                    a += 1
                if (b - a) // 2 >= 2:
                    n = (b - a) // 2
                    with pe.Fori(0, n) as i:
                        group(kind, G + a, h + 8 * a, i=i)
                        group(kind, G + a + 1, h + 8 * a + 8, i=i)
                    a += 2 * n
                for g in range(a, b):
                    group(kind, G + g, h + 8 * g)

            def sums(name):
                for q, (g, _, n, start, stop) in enumerate(quads_of(NORM_GROUPS[name])):
                    k = SQ0[name] + q
                    pe.wait_ge(sq_ready, k + 1)
                    for j in range(n):
                        mm = pe.matmul(ps[:, 4 + g // 2, (g % 2) * S:(g % 2) * S + S], ones[:, :],
                                       sq[:, k % 2, j * S:(j + 1) * S], start=start and j == 0,
                                       stop=stop and j == n - 1, skip_group_check=True)
                    mm.then_inc(sq_used, 1)

            def ada_sum(s):
                pe.wait_ge(ada_used, 32 * (s + 1))
                if s:
                    pe.wait_ge(mod_ready, s)
                for c in range(16):
                    mm = pe.matmul(ps[:, 7, c:c + 1], ada_acc[:, c * P:(c + 1) * P], ones[:, 0:1],
                                   start=True, stop=True, skip_group_check=True)
                mm.then_inc(ada_summed, 1)

            ident = const("ident")
            pe.wait_ge(ones_ready, 1)
            pe.wait_ge(s_const, 16)
            pe.wait_ge(rel_landed, 32)
            pe.matmul(ps[0:8, 5, 0:S], work[0:32, 2560:2568], work[0:32, 2048:2048 + S],
                      start=True, stop=True).then_inc(rel_ps, 1)
            sums("mem")
            groups("T", "xk", 0, 4, al=0)
            ada_sum(0)
            groups("N", "xv", 0, 4)
            ada_sum(1)
            sums("mix")
            groups("T", "win", 0, 4, al=al_before("mix"))
            ada_sum(2)
            groups("N", "win", 4, 6)
            groups("T", "win", 6, 8)
            ada_sum(3)
            groups("T", "win", 8, 11)
            G, h = G0["dt"], H0["dt"]
            pe.wait_ge(evac[G % 2], G // 2)
            wait_half(h + 2)
            for t in range(2):
                for k in range(16):
                    a = slice(t * P, (t + 1) * P)
                    w = slice(k * 16, (k + 1) * 16)
                    o = acc_tok(G)[:, t, 0:16]
                    pe.matmul(o, a_hi[:, k, a], w_hi[:, h % 4, w], start=k == 0, stop=False,
                              skip_group_check=True)
                    pe.matmul(o, a_lo[:, k, a], w_hi[:, h % 4, w], start=False, stop=False,
                              skip_group_check=True)
                    mm = pe.matmul(o, a_hi[:, k, a], w_lo[:, h % 4, w], start=False, stop=k == 15,
                                   skip_group_check=True)
            mm.then_inc(half_used, 2)
            ada_sum(4)

            def attention(kind, q_of, k_of, v, chunks=1, rope=None):
                u0 = HEADS[kind]
                n = XH if kind == "x" else NH

                def scores(u):
                    h = u - u0
                    if u >= 2:
                        pe.wait_ge(exp_done, u - 1)
                    for qt in range(2):
                        o = ps[:, 4 + u % 2, qt * S:(qt + 1) * S]
                        a = slice(qt * P, (qt + 1) * P)
                        for c in range(chunks):
                            mm = pe.matmul(o, q_of(h, c)[:, a], k_of(h, c), start=c == 0,
                                           stop=c == chunks - 1 and rope is None, skip_group_check=True)
                        if rope is not None:
                            lo, qr, kr = rope(h)
                            mm = pe.matmul(o, qr[lo:lo + 64, a], kr[lo:lo + 64, :], start=False, stop=True,
                                           skip_group_check=True)
                    mm.then_inc(s_ready, 1)

                def turn(u):
                    pe.wait_ge(p_ready, u + 1)
                    if u >= 2:
                        pe.wait_ge(pt_copied, u - 1)
                    for kt in range(2):
                        for qt in range(2):
                            mm = pe.transpose(ps[:, 6 + u % 2, kt * S + qt * P:kt * S + (qt + 1) * P],
                                              prob[:, u % 2, qt * S + kt * P:qt * S + (kt + 1) * P], ident)
                    mm.then_inc(pt_ready, 1)

                def values(u):
                    h = u - u0
                    pe.wait_ge(pt_copied, u + 1)
                    if u >= 2:
                        pe.wait_ge(o_evac, u - 1)
                    for c in range(chunks):
                        o = ps[:, 2 * (u % 2) + c // 2, (c % 2) * S:(c % 2) * S + S]
                        for kt in range(2):
                            w = slice((h * chunks + c) * P, (h * chunks + c + 1) * P)
                            mm = pe.matmul(o, v[:, kt, w], probT[:, u % 2, kt * S:(kt + 1) * S],
                                           start=kt == 0, stop=kt == 1, skip_group_check=True)
                    mm.then_inc(o_ready, 1)

                scores(u0)
                for u in range(u0, u0 + n):
                    if u + 1 < u0 + n:
                        scores(u + 1)
                    turn(u)
                    if u > u0:
                        values(u - 1)
                values(u0 + n - 1)

            for g in range(4, 6):
                G = G0["win"] + g
                pe.wait_ge(evac[G % 2], G // 2 + 1)
            G = G0["dt"]
            pe.wait_ge(evac[G % 2], G // 2 + 1)
            attention("moba", lambda h, c: q_r[:, h, :], lambda h, c: k_r[:, h, :], v_r)

            pe.wait_ge(silu_ready, 3)
            pe.wait_ge(o_evac, 8)
            for t in range(2):
                for hf in range(2):
                    for c in range(4):
                        mm = pe.transpose(ps[:, 2 * t + hf, c * P:(c + 1) * P],
                                          xs_r[:, 4 * hf + c, t * P:(t + 1) * P], ident)
                    mm.then_inc(xt_ready, 1)
            pe.wait_ge(exp_done, 8)
            for g in range(2):
                pe.matmul(ps[:, 4 + g, 0:S], bc_r[:, g, 0:P], bc_r[:, 2 + g, :], start=True, stop=True,
                          skip_group_check=True)
                pe.matmul(ps[:, 4 + g, S:S + P], bc_r[:, g, P:S], bc_r[:, 2 + g, P:S], start=True,
                          stop=True, skip_group_check=True).then_inc(gram_ready, 1)
            tri, after = const("tri"), const("after")

            def segment(h):
                pe.wait_ge(seg_ready, h + 1)
                if h >= 2:
                    pe.wait_ge(decay_ready, h - 1)
                else:
                    pe.wait_ge(pt_copied, 7 + h)
                o = ps[:, 6 + h % 2, :]
                r = seg_in[:, h % 2, :]
                pe.matmul(o[:, 0:S], after, r[:, 0:S], start=True, stop=False, skip_group_check=True)
                pe.matmul(o[:, P:S], ones[:, :], r[:, S:S + P], start=False, stop=True,
                          skip_group_check=True)
                pe.matmul(o[:, S:S + P], after, r[:, S:S + P], start=True, stop=True,
                          skip_group_check=True).then_inc(seg_summed, 1)

            def state_out(h):
                pe.wait_ge(m_ready, h + 1)
                c, lo = h // 2, 64 * (h % 2)
                if h == 0:
                    pe.wait_ge(xt_copied, 4)
                if h % 2 == 0 and c >= 2:
                    pe.wait_ge(y_done, c - 1)
                o = ps[lo:lo + 64, c % 2, 0:S]
                w = slice(h * 64, (h + 1) * 64)
                m = mix_m[:, h % 2, :]
                pe.matmul(o, xtok[:, 0, w], m[:, 0:S], start=True, stop=False, skip_group_check=True)
                pe.matmul(o[:, P:S], xtok[:, 1, w], m[:, S:S + P], start=False, stop=True,
                          skip_group_check=True).then_inc(y_ready, 1)

            segment(0)
            for h in range(STATE_HEADS):
                if h + 1 < STATE_HEADS:
                    segment(h + 1)
                state_out(h)

            sums("mixin")
            pe.wait_ge(y_done, 8)
            groups("T", "wout", 0, 4, al=al_before("mixin"))
            ada_sum(5)
            sums("ffn")
            groups("T", "up", 0, 22, al=al_before("ffn"))

            def down(name, hs0):
                G, base = G0[name], H0[name]
                outs = [[acc(G), acc(G + 1)], [acc_b(0), acc_b(1)]]
                sets = [G % 2, (G + 1) % 2]

                def step(half, n, i, first, last):
                    par = n % 2
                    base_n = base + 4 * n
                    pe.wait_ge(hl_ready, hs0 + n + 1 if i is None else i * 2 + (hs0 + n + 1))
                    for s in range(4):
                        cg, kp = s // 2, s % 2
                        if first and kp == 0 and half == 0:
                            pe.wait_ge(evac[sets[cg]], (G + cg) // 2)
                        wait_half(base_n + s + 1 if i is None else i * 8 + (base_n + s + 1))
                        half_T((base_n + s) % 4, outs[half][cg], par * 4 + 2 * kp, first and kp == 0,
                               last and kp == 1)

                for half in range(2):
                    n0 = 11 * half
                    step(half, n0, None, True, False)
                    with pe.Fori(0, 5) as i:
                        step(half, n0 + 1, i, False, False)
                        step(half, n0 + 2, i, False, False)

            down("down", 0)

            pe.wait_ge(evac_b, 2)
            sums("fin")
            sums("lnmix")

            groups("T", "win2", 0, 4, al=al_before("lnmix"))
            groups("N", "win2", 4, 6)
            group("T", G0["win2"] + 6, H0["win2"] + 48)
            group("T", G0["win2"] + 7, H0["win2"] + 56, chunks=3)
            sums("qkv")
            a0, lat = al_before("qkv"), H0["uq"]
            for g in range(3):
                G = G0["uq"] + g
                pe.wait_ge(evac[G % 2], G // 2)
                for s in range(2):
                    wait_half(lat + 2 * g + s + 1)
                    if g == 0:
                        al_quad(a0 + 1)
                    half_T((lat + 2 * g + s) % 4, acc(G), 2 * s, s == 0, s == 1)
            for g in range(4):
                G = G0["ukv"] + g
                pe.wait_ge(evac[G % 2], G // 2)
                wait_half(lat + 6 + g + 1)
                if g == 0:
                    al_quad(a0 + 2)
                if g < 2:
                    half_T((lat + 6 + g) % 4, acc(G), 4, True, True)
                else:
                    half_N((lat + 6 + g) % 4, acc_tok(G), 4, True, True)
            G = G0["ukv"] + 3
            pe.wait_ge(evac[G % 2], G // 2 + 1)
            pe.wait_ge(evac[(G + 1) % 2], (G + 1) // 2)
            for j, c in enumerate([0, 1, 2, 3, 6]):
                if j:
                    pe.wait_ge(rot_done, j)
                pe.matmul(ps[:, 5, 0:S], const("rot"), ckv_r[:, c, :], start=True, stop=True,
                          skip_group_check=True).then_inc(rot_ready, 1)
            pe.wait_ge(rot_done, 5)
            attention("na", lambda h, c: q_r[:, h, :], lambda h, c: k_r[:, h, :], v_r)
            attention("mla", lambda h, c: qn_r[:, h, :], lambda h, c: kn_r[:, h, :], v2_r,
                      rope=lambda h: (64 * (h % 2), ckv_r[:, h // 2, :], ckv_r[:, 6, :]))
            sums("mixin2")
            pe.wait_ge(o_evac, 24)
            groups("T", "wout2", 0, 4, al=al_before("mixin2"))
            sums("lnmem")
            groups("T", "xq", 0, 4, al=al_before("lnmem"))
            for g in range(2, 4):
                G = G0["xq"] + g
                pe.wait_ge(evac[G % 2], G // 2 + 1)
            pe.wait_ge(reload_done, 128)
            attention("x", lambda h, c: qx_r[:, 4 * h + c, :], lambda h, c: kx_r[:, 4 * h + c, :], vx_r,
                      chunks=4)
            pe.wait_ge(o_evac, 28)
            groups("T", "xo", 0, 4, al=al_before("xo"))
            sums("lnffn")
            groups("T", "gu", 0, 22, al=al_before("lnffn"))
            down("down2", 22)
            pe.wait_ge(evac_b, 4)
            sums("fin2")

        @block.vector
        def _(dve):
            steps = [0]

            def link(ins):
                steps[0] += 1
                ins.then_inc(dve_step, 1)

            def settle(extra=None):
                dve.wait_ge(dve_step, steps[0] if extra is None else extra + steps[0])

            def chunked(ap):
                return ap.rearrange("p (c t) -> p c t", t=S)

            def ada_unit(u):
                s, k4 = u // 4, u % 4
                if k4 == 0 and s:
                    dve.wait_ge(ada_summed, s)
                for i in range(8):
                    n = 8 * u + i
                    dve.wait_ge(ada_landed[i % 2], 16 * (n // 2 + 1))
                    k, part = 4 * k4 + i // 2, i % 2
                    a = ada_acc[:, part * 1024:(part + 1) * 1024]
                    ck = small[:, 16 + k:17 + k]
                    if k == 0:
                        ins = dve.tensor_scalar(a, ada_ring[:, i % 2], ck, None, ALU.mult)
                    else:
                        dve.wait_ge(ada_used, n - 1)
                        ins = dve.scalar_tensor_tensor(out=a, in0=ada_ring[:, i % 2], scalar=ck, in1=a,
                                                       op0=ALU.mult, op1=ALU.add)
                    ins.then_inc(ada_used, 1)

            def ada_mod(s):
                dve.wait_ge(ada_summed, s + 1)
                sl = ADA_ORDER[s]
                dve.tensor_tensor(mod[:, s, :], ps[:, 7, 0:16], col("b_ada", 16 * sl, 16), ALU.add)\
                   .then_inc(mod_ready, 1)
                dve.wait_ge(mod_ready, s + 1)
                if sl in (1, 4):
                    g = col("mix_g" if sl == 1 else "ffn_g", 0, 16)
                    link(dve.scalar_tensor_tensor(out=mod[:, s, :], in0=mod[:, s, :], scalar=1.0, in1=g,
                                                  op0=ALU.add, op1=ALU.mult))
                    settle()

            def newton(name):
                groups = NORM_GROUPS[name]
                dve.wait_ge(sq_used, SQ0[name] + len(quads_of(groups)))
                w = len(groups) * S
                v, u, y = work[:, 0:w], work[:, 768:768 + w], rstd[:, 0:w]
                for g, (_, width) in enumerate(groups):
                    link(dve.tensor_scalar(v[:, g * S:(g + 1) * S],
                                           ps[:, 4 + g // 2, (g % 2) * S:(g % 2) * S + S],
                                           1.0 / width, EPS,
                                           ALU.mult, ALU.add))
                settle()
                link(dve.tensor_scalar(u.bitcast(I32), v.bitcast(I32), 1, None, ALU.logical_shift_right))
                settle()
                link(dve.tensor_scalar(y.bitcast(I32), u.bitcast(I32), -1.0, float(0x5F3759DF), ALU.mult,
                                       ALU.add))
                settle()
                for _ in range(3):
                    link(dve.scalar_tensor_tensor(out=u, in0=y, scalar=-0.5, in1=v, op0=ALU.mult,
                                                  op1=ALU.mult))
                    settle()
                    link(dve.tensor_tensor(u, u, y, ALU.mult))
                    settle()
                    link(dve.scalar_tensor_tensor(out=y, in0=u, scalar=1.5, in1=y, op0=ALU.add,
                                                  op1=ALU.mult))
                    settle()

            def norm(name, source, gain, shift=None):
                newton(name)
                first = al_before(name)
                t0 = tmp_at(first)
                quads = quads_of(NORM_GROUPS[name])

                def low(q):
                    _, c, n, _, _ = quads[q]
                    dve.wait_ge(ah_ready, first + q + 1)
                    dve.tensor_tensor(a_lo[:, c:c + n, :], chunked(tmp[:, (t0 + q) % 2, 0:n * S]),
                                      a_hi[:, c:c + n, :].bitcast(F32), ALU.subtract).then_inc(al_ready, 1)

                for q, (g, c, n, _, _) in enumerate(quads):
                    if first + q >= 2:
                        dve.wait_ge(al_ready, max(first + q - 1, first))
                    for j in range(n):
                        o = tmp[:, (t0 + q) % 2, j * S:(j + 1) * S]
                        ins = dve.scalar_tensor_tensor(out=o, in0=source(c + j), scalar=gain(c + j),
                                                       in1=rstd[:, g * S:(g + 1) * S], op0=ALU.mult,
                                                       op1=ALU.mult)
                        if shift is not None:
                            link(ins)
                    if shift is not None:
                        settle()
                        for j in range(n):
                            o = tmp[:, (t0 + q) % 2, j * S:(j + 1) * S]
                            ins = dve.tensor_scalar(o, o, shift(c + j), None, ALU.add)
                    ins.then_inc(tmp_ready, 1)
                    dve.wait_ge(tmp_ready, t0 + q + 1)
                    if q:
                        low(q - 1)
                low(len(quads) - 1)

            def norm_in_place(name, gain, signal):
                newton(name)
                for c in range(16):
                    ins = dve.scalar_tensor_tensor(out=res[:, c, :], in0=res[:, c, :], scalar=gain(c),
                                                   in1=rstd[:, 0:S], op0=ALU.mult, op1=ALU.mult)
                    if c % 4 == 3:
                        ins.then_inc(signal, 1)
                return signal

            def residual(q, src, halves, signal, gate=None):
                dve.wait_ge(half_used, halves)
                r = res[:, 4 * q:4 * q + 4, :]
                if gate is None:
                    ins = dve.tensor_tensor(r, src, r, ALU.add)
                else:
                    for j in range(4):
                        ins = dve.scalar_tensor_tensor(out=r[:, j, :], in0=src[:, j, :],
                                                       scalar=mod[:, gate, 4 * q + j:4 * q + j + 1],
                                                       in1=r[:, j, :], op0=ALU.mult, op1=ALU.add)
                ins.then_inc(signal, 1)

            def residual_groups(name, gate=None, between=None):
                for g in range(4):
                    if between is not None:
                        between(g)
                    G = G0[name] + g
                    residual(g, acc(G), H0[name] + 8 * g + 8, evac[G % 2], gate)

            def down(name, hs0, gate=None):
                for n in range(22):
                    dve.wait_ge(hs_ready, hs0 + n + 1)
                    quad, a = n % 11, (n % 2) * 4
                    dve.tensor_tensor(a_lo[:, a:a + 4, :], hidden[:, 4 * quad:4 * quad + 4, :],
                                      a_hi[:, a:a + 4, :].bitcast(F32), ALU.subtract).then_inc(hl_ready, 1)
                    if n == 12:
                        for c in range(2):
                            G = G0[name] + c
                            residual(c, acc(G), H0[name] + 44, evac[G % 2], gate)
                for c in range(2):
                    residual(2 + c, acc_b(c), H0[name] + 88, evac_b, gate)

            def convolve(dst, src, w, b, taps, signal, extra=None):
                for c in range(4):
                    link(dve.tensor_scalar(dst[:, c, :], src[:, c, :], w(c, taps - 1), b(c), ALU.mult,
                                           ALU.add))
                for shift in range(1, taps):
                    settle(extra)
                    for c in range(4):
                        ins = dve.scalar_tensor_tensor(out=dst[:, c, shift:S], in0=src[:, c, 0:S - shift],
                                                       scalar=w(c, taps - 1 - shift),
                                                       in1=dst[:, c, shift:S], op0=ALU.mult, op1=ALU.add)
                        if shift < taps - 1:
                            link(ins)
                ins.then_inc(signal, 1)

            def conv_ssm(g, j, par):
                G = G0["win"] + g
                dve.wait_ge(half_used, H0["win"] + 8 * g + 8)
                if j == 2:
                    dve.wait_ge(silu_ready, 1)
                convolve(conv[:, par], acc(G), lambda c, t: col("cs_w", 4 * (4 * j + c) + t),
                         lambda c: col("cs_b", 4 * j + c), 4, evac[G % 2])

            def attention(kind, scale):
                u0 = HEADS[kind]
                n = XH if kind == "x" else NH
                biased = kind in ("moba", "na")

                def front(u):
                    dve.wait_ge(s_ready, u + 1)
                    src = ps[:, 4 + u % 2, :]
                    neg = small[:, 4 * (u % 2):4 * (u % 2) + 2]
                    if biased:
                        landed = 32 * (u // 2 + 1) if kind == "moba" else 128 + 64 * ((u - u0) // 2 + 1)
                        dve.wait_ge(bias_landed[u % 2], landed)
                        b = bias[:, u % 2, :]
                        if kind == "na":
                            b3 = b.rearrange("p (r c) -> p r c", c=GRID)
                            link(dve.tensor_tensor(b3, b3, const("window").unsqueeze(1).broadcast_to([P, 8, GRID]),
                                                   ALU.add))
                            settle()
                        link(dve.scalar_tensor_tensor(out=logit[:, u % 2, :], in0=src, scalar=scale, in1=b,
                                                      op0=ALU.mult, op1=ALU.add))
                        settle()
                        src = logit[:, u % 2, :]
                    ins = dve.tensor_reduce(neg, src.rearrange("p (q k) -> p q k", q=2), AX_X, ALU.max,
                                            negate=True)
                    if not biased:
                        link(ins)
                        settle()
                        ins = dve.tensor_scalar(neg, neg, scale, None, ALU.mult)
                    ins.then_inc(max_ready, 1)

                def back(u):
                    dve.wait_ge(exp_done, u + 1)
                    r = small[:, 32 + 2 * (u % 2):34 + 2 * (u % 2)]
                    link(dve.reciprocal(r, small[:, 8 + 4 * (u % 2):10 + 4 * (u % 2)]))
                    settle()
                    for qt in range(2):
                        o = prob[:, u % 2, qt * S:(qt + 1) * S]
                        ins = dve.tensor_scalar(o, o, r[:, qt:qt + 1], None, ALU.mult)
                    ins.then_inc(p_ready, 1)

                front(u0)
                for u in range(u0, u0 + n):
                    if u + 1 < u0 + n:
                        front(u + 1)
                    back(u)

            dve.memset(work[0:56, 3328:3328 + P], 0.0).then_inc(rpb_zero, 1)
            link(dve.memset(work[0:8, 2568 + S:2568 + REL], MASKED))
            dve.wait_ge(rel_ps, 1)
            settle()
            dve.tensor_copy(work[0:8, 2568:2568 + S], ps[0:8, 5, 0:S]).then_inc(rel_row, 1)
            dve.wait_ge(s_vec, 16)
            dve.wait_ge(s_mem, 16)
            dve.wait_ge(scr_stored, 32)
            memory = region(0, 16)
            norm("mem", lambda c: memory[:, c, :], lambda c: col("mem_g", c))
            dve.wait_ge(c_ready, 1)
            for u in range(8):
                if u == 4:
                    ada_mod(0)
                ada_unit(u)
            ada_mod(1)

            dve.wait_ge(s_const, 16)
            norm("mix", lambda c: res[:, c, :], lambda c: mod[:, 0, c:c + 1], lambda c: mod[:, 1, c:c + 1])
            for g in range(12):
                if g in (4, 8):
                    ada_mod(g // 4 + 1)
                ada_unit(8 + g)
                if g == 7:
                    conv_ssm(6, 0, 0)
                if g == 8:
                    conv_ssm(7, 1, 1)
                if g == 11:
                    conv_ssm(10, 2, 0)
            ada_mod(4)
            G = G0["dt"]
            dve.wait_ge(half_used, H0["dt"] + 2)
            for t in range(2):
                ins = dve.tensor_tensor(dts[:, 0, 16 * t:16 * t + 16], acc_tok(G)[:, t, 0:16],
                                        col("dtb", 0, 16), ALU.add)
            ins.then_inc(evac[G % 2], 1)
            dve.wait_ge(evac[G % 2], G // 2 + 1)
            dve.scalar_tensor_tensor(out=dts[:, 1, :], in0=dts[:, 0, :], scalar=-1.0, in1=dts[:, 0, :],
                                     op0=ALU.mult, op1=ALU.min).then_inc(dt_done, 1)
            attention("moba", HD ** -0.5)

            e, s_, z2, p_ = dts[:, 2, :], dts[:, 6, :], dts[:, 7, :], dts[:, 8, :]
            dve.wait_ge(dt_exp, 1)
            link(dve.tensor_scalar(dts[:, 4, :], e, 2.0, None, ALU.add))
            link(dve.tensor_scalar(dts[:, 9, :], dts[:, 0, :], 0.0, None, ALU.max))
            settle()
            link(dve.reciprocal(dts[:, 5, :], dts[:, 4, :]))
            settle()
            link(dve.tensor_tensor(s_, e, dts[:, 5, :], ALU.mult))
            settle()
            link(dve.tensor_tensor(z2, s_, s_, ALU.mult))
            settle()
            link(dve.tensor_scalar(p_, z2, 1.0 / 15, None, ALU.mult))
            for k in (13, 11, 9, 7, 5, 3):
                settle()
                link(dve.scalar_tensor_tensor(out=p_, in0=p_, scalar=1.0 / k, in1=z2, op0=ALU.add,
                                              op1=ALU.mult))
            settle()
            link(dve.scalar_tensor_tensor(out=p_, in0=p_, scalar=1.0, in1=s_, op0=ALU.add, op1=ALU.mult))
            settle()
            link(dve.scalar_tensor_tensor(out=dts[:, 10, :], in0=p_, scalar=2.0, in1=dts[:, 9, :],
                                          op0=ALU.mult, op1=ALU.add))
            settle()
            for t in range(2):
                link(dve.scalar_tensor_tensor(out=dts[:, 11, 16 * t:16 * t + 16],
                                              in0=dts[:, 10, 16 * t:16 * t + 16], scalar=-1.0,
                                              in1=dts[:, 3, 0:16], op0=ALU.mult, op1=ALU.mult))
            settle()

            tri = const("tri")
            dve.wait_ge(gram_ready, 2)
            for g in range(2):
                dve.tensor_tensor(gram[:, g, 0:S], ps[:, 4 + g, 0:S], tri, ALU.mult)
                link(dve.tensor_tensor(gram[:, g, S:S + P], ps[:, 4 + g, S:S + P], tri[:, 0:P], ALU.mult))
            settle()

            def seg(h):
                if h >= 2:
                    dve.wait_ge(seg_summed, h - 1)
                r = seg_in[:, h % 2, :]
                dve.tensor_scalar(r[:, 0:S], tri, dts[:, 11, h:h + 1], None, ALU.mult)
                dve.tensor_scalar(r[:, S:S + P], tri[:, 0:P], dts[:, 11, 16 + h:17 + h], None, ALU.mult)\
                   .then_inc(seg_ready, 1)

            def mixing(h):
                dve.wait_ge(decay_ready, h + 1)
                if h >= 2:
                    dve.wait_ge(y_ready, h - 1)
                for t, (a, b) in enumerate([(0, S), (S, S + P)]):
                    ins = dve.scalar_tensor_tensor(out=mix_m[:, h % 2, a:b], in0=decay[:, h % 2, a:b],
                                                   scalar=dts[:, 10, 16 * t + h:16 * t + h + 1],
                                                   in1=gram[:, h // 8, a:b], op0=ALU.mult, op1=ALU.mult)
                ins.then_inc(m_ready, 1)

            def gate_y(c):
                dve.wait_ge(y_ready, 2 * c + 2)
                o = work[:, 3072 + (c % 2) * S:3072 + (c % 2 + 1) * S]
                link(dve.scalar_tensor_tensor(out=o, in0=xs_r[:, c, :], scalar=col("dskip", c),
                                              in1=ps[:, c % 2, 0:S], op0=ALU.mult, op1=ALU.add))
                settle()
                dve.tensor_tensor(z_r[:, c, :], o, z_r[:, c, :], ALU.mult).then_inc(y_done, 1)

            seg(0)
            seg(1)
            for h in range(STATE_HEADS):
                mixing(h)
                if h + 2 < STATE_HEADS:
                    seg(h + 2)
                if h % 2 == 0 and h:
                    gate_y(h // 2 - 1)
            gate_y(7)
            dve.wait_ge(y_done, 8)

            norm("mixin", lambda c: q_r[:, c, :] if c < 8 else z_r[:, c - 8, :],
                 lambda c: col("attn_g", c) if c < 8 else col("ssm_g", c - 8))
            residual_groups("wout", gate=2, between=lambda g: ada_unit(20 + g))
            ada_mod(5)
            norm("ffn", lambda c: res[:, c, :], lambda c: mod[:, 3, c:c + 1], lambda c: mod[:, 4, c:c + 1])

            def up_conv(g, i=None, extra=None):
                G = G0["up"] + g
                base = H0["up"] + 8 * g + 8
                dve.wait_ge(half_used, base if i is None else i * 16 + base)
                if i is not None:
                    dve.wait_ge(hid_ready, i * 2 + (g - 1))

                def column(name, n, k):
                    if i is None:
                        return col(name, n)
                    return vec[:, bass.ds(i * k + (V0[name] + n), 1)]

                convolve(conv[:, g % 2], acc(G), lambda c, t: column("cf_w", 12 * g + 3 * c + t, 24),
                         lambda c: column("cf_b", 4 * g + c, 8), 3, evac[G % 2], extra)

            def up_gate(g, i=None):
                base = 3 + g + 1
                dve.wait_ge(silu_ready, base if i is None else i * 2 + base)
                o = hidden[:, 2 * g:2 * g + 2, :] if i is None else hidden[:, bass.ds(i * 4 + 2 * g, 2), :]
                dve.tensor_tensor(o, conv[:, g % 2, 0:2, :], conv[:, g % 2, 2:4, :], ALU.mult)\
                   .then_inc(hid_ready, 1)

            up_conv(0)
            up_conv(1)
            up_gate(0)
            PER_TURN = 16
            with dve.Fori(0, 10) as i:
                before = steps[0]
                for p in range(2):
                    up_conv(2 + p, i, i * PER_TURN)
                    up_gate(1 + p, i)
                assert steps[0] - before == PER_TURN
            steps[0] += 9 * PER_TURN
            up_gate(21)
            down("down", 0, gate=5)

            norm_in_place("fin", lambda c: col("fin_g", c), res_ready)
            dve.wait_ge(res_ready, 4)
            norm("lnmix", lambda c: res[:, c, :], lambda c: col("lnmix_g", c))
            for q in range(2):
                G = G0["win2"] + 6 + q
                dve.wait_ge(evac[G % 2], G // 2 + 1)
            norm("qkv", lambda c: ckv_r[:, c, :], lambda c: col("q_g", c) if c < 4 else col("kv_g", c - 4))

            G = G0["uq"] + 2
            dve.wait_ge(evac[G % 2], G // 2 + 1)
            for j, c in enumerate([0, 1, 2, 3, 6]):
                dve.wait_ge(rot_ready, j + 1)
                o = work[:, 3584:3584 + S]
                link(dve.tensor_tensor(o, ps[:, 5, 0:S], const("sin"), ALU.mult))
                link(dve.tensor_tensor(ckv_r[:, c, :], ckv_r[:, c, :], const("cos"), ALU.mult))
                settle()
                dve.tensor_tensor(ckv_r[:, c, :], ckv_r[:, c, :], o, ALU.add).then_inc(rot_done, 1)
                dve.wait_ge(rot_done, j + 1)
            attention("na", HD ** -0.5)
            attention("mla", 192 ** -0.5)
            dve.wait_ge(o_evac, 24)
            norm("mixin2", lambda c: q_r[:, c, :] if c < 8 else qn_r[:, c - 8, :],
                 lambda c: col("na_g", c) if c < 8 else col("mla_g", c - 8))
            residual_groups("wout2")
            for g in range(4):
                G = G0["wout2"] + g
                dve.wait_ge(evac[G % 2], G // 2 + 1)
            norm("lnmem", lambda c: res[:, c, :], lambda c: col("lnmem_g", c))
            attention("x", 512 ** -0.5)
            for q in range(4):
                dve.wait_ge(ah_ready, al_before("xo") + q + 1)
                dve.tensor_tensor(a_lo[:, 4 * q:4 * q + 4, :], qx_r[:, 4 * q:4 * q + 4, :],
                                  a_hi[:, 4 * q:4 * q + 4, :].bitcast(F32), ALU.subtract)\
                   .then_inc(al_ready, 1)
            residual_groups("xo")
            for g in range(4):
                G = G0["xo"] + g
                dve.wait_ge(evac[G % 2], G // 2 + 1)
            norm("lnffn", lambda c: res[:, c, :], lambda c: col("lnffn_g", c))

            def swiglu(g, i=None):
                G, base = G0["gu"] + g, 25 + g + 1
                dve.wait_ge(silu_ready, base if i is None else i * 2 + base)
                o = hidden[:, 2 * g:2 * g + 2, :] if i is None else hidden[:, bass.ds(i * 4 + 2 * g, 2), :]
                dve.tensor_tensor(o, acc(G)[:, 2:4, :], conv[:, g % 2, 0:2, :], ALU.mult)\
                   .then_inc(evac[G % 2], 1)

            swiglu(0)
            with dve.Fori(0, 10) as i:
                for p in range(2):
                    swiglu(1 + p, i)
            swiglu(21)
            down("down2", 22)
            norm_in_place("fin2", lambda c: col("fin2_g", c), out_ready)


def _tiles(w, cols=512, chunks=4):
    k, n = w.shape
    w = w.reshape(k // (P * chunks), chunks, P, n // cols, cols)
    return w.transpose(3, 0, 2, 1, 4).reshape(-1, P, chunks * cols)


def _down_tiles(w):
    w = w.reshape(11, 4, P, 2, 2, 512)
    return w.transpose(3, 0, 4, 2, 1, 5).reshape(-1, P, TILE)


def _pairs(gate, value):
    k = gate.shape[0]
    both = np.stack([gate.reshape(k, -1, 256), value.reshape(k, -1, 256)], axis=2)
    return both.reshape(k, -1)


def _cols(v, width=P):
    return np.asarray(v).reshape(-1, width).T


def _constants():
    p = np.arange(P)
    tri = (p[:, None] <= np.arange(S)[None, :]).astype(np.float32)
    after = (p[:, None] > p[None, :]).astype(np.float32)
    ident = np.eye(P, dtype=np.float32)
    inv = (1.0 / (np.float32(10000.0) ** (np.arange(0, 64, 2, dtype=np.float32) / np.float32(64)))).astype(np.float32)
    ang = np.arange(S, dtype=np.float32)[None, :] * inv[:, None]
    cos, sin = np.tile(np.cos(ang), (4, 1)), np.tile(np.sin(ang), (4, 1))
    rot = np.zeros((P, P), np.float32)
    for m in range(P):
        if m % 64 < 32:
            rot[m + 32, m] = -1.0
        else:
            rot[m - 32, m] = 1.0
    c = p % GRID
    start = np.clip(c - 8, 0, GRID - 16)
    k = np.arange(GRID)[None, :]
    window = np.where((k >= start[:, None]) & (k < start[:, None] + 16), 0.0, MASKED)
    consts = np.concatenate([tri, after, ident, cos, sin, rot, window], axis=1).astype(np.float32)
    dist = 255 - np.arange(S)
    nf = np.maximum(dist, 16).astype(np.float32)
    large = 16 + (np.log(nf / np.float32(16)) / np.float32(np.log(8.0)) * np.float32(16)).astype(np.int32)
    bucket = np.where(dist < 16, dist, np.minimum(large, 31))
    onehot = np.zeros((32, 512), np.float32)
    onehot[bucket, np.arange(S)] = 1.0
    return consts, onehot


def _layout(a):
    w_in = a["w_in"][0]
    dt = np.zeros((P, TILE), np.float32)
    dt[:, 0:256] = w_in[:, 5632:5648].reshape(16, P, 16).transpose(1, 0, 2).reshape(P, 256)
    w_in2 = a["w_in_2"][0]
    rope = w_in2[:, 3840:3904]
    w_in2 = np.concatenate([w_in2[:, 0:3840], rope, rope, rope, rope], axis=1)
    uq = a["w_uq_2"][0].reshape(512, NH, 192)
    uq = np.concatenate([uq[:, :, 0:128].reshape(512, -1), uq[:, :, 128:].reshape(512, -1)], axis=1)
    ukv = a["w_ukv_2"][0].reshape(256, NH, 256)
    ukv = np.concatenate([ukv[:, :, 0:128].reshape(256, -1), ukv[:, :, 128:].reshape(256, -1)], axis=1)
    ukv = _tiles(ukv, 512, 2).reshape(2, 2, P, HALF).transpose(0, 2, 1, 3).reshape(2, P, TILE)
    up = a["w_up"][0]
    stream = np.concatenate([
        _tiles(a["w_xk_2"][0]), _tiles(a["w_xv_2"][0]), _tiles(w_in[:, 0:5632]), dt[None],
        _tiles(a["w_out"][0]), _tiles(_pairs(up[:, :FF], up[:, FF:])), _down_tiles(a["w_down"][0]),
        _tiles(w_in2), _tiles(uq), ukv, _tiles(a["w_out_2"][0]), _tiles(a["w_xq_2"][0]),
        _tiles(a["w_xo_2"][0]), _tiles(_pairs(a["w_gate_2"][0], a["w_up_2"][0])),
        _down_tiles(a["w_down_2"][0])])
    ada = a["w_ada"][0].reshape(16, P, 6, 2, 1024)[:, :, ADA_ORDER]
    ada = ada.transpose(2, 0, 3, 1, 4).reshape(-1, P, 1024)
    cw, cb = a["conv_ffn_w"][0], a["conv_ffn_b"][0]
    cfw = _pairs(cw[:, :FF], cw[:, FF:]).reshape(3, 88, P).transpose(2, 1, 0).reshape(P, 264)
    cfb = _cols(_pairs(cb[None, :FF], cb[None, FF:]))
    csw = a["conv_ssm_w"][0].reshape(4, 12, P).transpose(2, 1, 0).reshape(P, 48)
    parts = {"c": _cols(a["c"][0]), "b_ada": _cols(a["b_ada"][0]), "mix_g": _cols(a["norm_mix_g"][0]),
             "attn_g": _cols(a["attn_norm_g"][0]), "ssm_g": _cols(a["ssm_norm_g"][0]), "cs_w": csw,
             "cs_b": _cols(a["conv_ssm_b"][0]), "dskip": _cols(np.repeat(a["d_skip"][0], 64)),
             "ffn_g": _cols(a["norm_ffn_g"][0]), "cf_b": cfb, "cf_w": cfw,
             "fin_g": _cols(a["final_norm_g"]), "lnmix_g": _cols(a["ln_mix_2"][0]),
             "q_g": _cols(a["q_norm_2"][0]), "kv_g": _cols(a["kv_norm_2"][0]),
             "na_g": _cols(a["na_out_norm_2"][0]), "mla_g": _cols(a["mla_out_norm_2"][0]),
             "lnmem_g": _cols(a["ln_mem_2"][0]), "mem_g": _cols(a["mem_norm_2"][0]),
             "lnffn_g": _cols(a["ln_ffn_2"][0]), "fin2_g": _cols(a["final_norm_2"]),
             "dtb": np.tile(a["dt_bias"][0], (P, 1)), "alog": np.tile(a["a_log"][0], (P, 1))}
    vecs = np.concatenate([parts[n] for n, _ in VEC], axis=1)
    assert vecs.shape == (P, NVEC)
    turned = lambda x: x[0].T.reshape(16, P, S).transpose(1, 0, 2)
    consts, onehot = _constants()
    return {"stream": stream, "ada": ada, "xT": turned(a["x"]), "memT": turned(a["mem_2"]), "vecs": vecs,
            "consts": consts, "onehot": onehot, "relb": a["rel_bias"],
            "rpb": a["na_rpb_2"][0][:, 4:11].reshape(56, 31)}


def kernel(**inputs):
    import concourse.bacc as _bacc
    from concourse.bass_utils import run_bass_kernel_spmd as _run

    a = {k: np.asarray(v) for k, v in inputs.items()}
    arrays = {k: np.ascontiguousarray(v) for k, v in _layout(a).items()}
    nc = _bacc.Bacc("TRN2", target_bir_lowering=False, num_devices=1)
    args = [nc.dram_tensor(k, v.shape, F32, kind="ExternalInput").ap() for k, v in arrays.items()]
    out = nc.dram_tensor("out", [P, 16, S], F32, kind="ExternalOutput").ap()
    scratch = [nc.dram_tensor(n, s, F32).ap() for n, s in
               [("rel_rows", [8, P, REL]), ("rpb_rows", [56, GRID, NA_W]), ("k_spill", [4, P, 1024]),
                ("v_spill", [4, P, 1024])]]
    block_program(nc, *args, out, *scratch)
    r = _run(nc, [arrays], core_ids=[0])
    got = r.results[0]["out"]
    return got.transpose(1, 0, 2).reshape(D, S).T.reshape(1, S, D)
```

```python
from contextlib import ExitStack

import numpy as np
import concourse.bass as bass
from concourse import mybir

F32 = mybir.dt.float32
F32R = mybir.dt.float32r
I32 = mybir.dt.int32
ALU = mybir.AluOpType
ACT = mybir.ActivationFunctionType
AX_X = mybir.AxisListType.X

P = 128
D = 2048
S = 256
FF = 5632
FC = FF // P
EPS = 1e-6
MASKED = -3.0e38
TILE = 2048
HALF = TILE // 2
RAW = 4
SLOTS = 4
HD = 128
NH = 8
XH = 4
STATE_HEADS = 16
REL = 512
NA_W = 127
GRID = 64

STREAM = [("xk", 16), ("win", 44), ("dt", 1), ("xv", 16), ("wout", 16), ("up", 88), ("down", 44),
          ("win2", 32), ("uq", 3), ("ukv", 2), ("wout2", 16), ("xq", 16), ("xo", 16), ("gu", 88),
          ("down2", 44)]
T0, _t = {}, 0
for _name, _n in STREAM:
    T0[_name] = _t
    _t += _n
TILES = _t
H0 = {k: 2 * v for k, v in T0.items()}

GROUPS = [("xk", 4), ("win", 11), ("dt", 1), ("xv", 4), ("wout", 4), ("up", 22), ("down", 2),
          ("win2", 8), ("uq", 3), ("ukv", 4), ("wout2", 4), ("xq", 4), ("xo", 4), ("gu", 22),
          ("down2", 2)]
G0, _g = {}, 0
for _name, _n in GROUPS:
    G0[_name] = _g
    _g += _n

ADA_ORDER = [1, 0, 2, 4, 3, 5]
ADA_UNITS = 4 * len(ADA_ORDER)

ADA_EARLY = 64

VEC = [("c", 16), ("b_ada", 96), ("mix_g", 16), ("attn_g", 8), ("ssm_g", 8), ("cs_w", 48),
       ("cs_b", 12), ("dskip", 8), ("ffn_g", 16), ("cf_b", 88), ("cf_w", 264),
       ("fin_g", 16), ("lnmix_g", 16), ("q_g", 4), ("kv_g", 2), ("na_g", 8), ("mla_g", 8),
       ("lnmem_g", 16), ("mem_g", 16), ("lnffn_g", 16), ("fin2_g", 16), ("dtb", 16), ("alog", 16)]
V0, _v = {}, 0
for _name, _n in VEC:
    V0[_name] = _v
    _v += _n
NVEC = _v

CONST = [("tri", 256), ("after", 128), ("ident", 128), ("cos", 256), ("sin", 256), ("rot", 128),
         ("window", 64)]
C0, _c = {}, 0
for _name, _n in CONST:
    C0[_name] = _c
    _c += _n
NCONST = _c

NORMS = [("mem", [(16, D)]), ("mix", [(16, D)]), ("mixin", [(8, 1024), (4, 512), (4, 512)]),
         ("ffn", [(16, D)]), ("fin", [(16, D)]), ("lnmix", [(16, D)]), ("qkv", [(4, 512), (2, 256)]),
         ("mixin2", [(8, 1024), (8, 1024)]), ("lnmem", [(16, D)]), ("lnffn", [(16, D)]),
         ("fin2", [(16, D)])]


def quads_of(groups):
    out, c = [], 0
    for g, (n, _) in enumerate(groups):
        for a in range(0, n, 4):
            out.append((g, c + a, min(4, n - a), a == 0, a + 4 >= n))
        c += n
    return out


SQ0, AL0, _q, _a = {}, {}, 0, 0
for _name, _groups in NORMS:
    SQ0[_name] = _q
    AL0[_name] = _a
    _q += len(quads_of(_groups))
    if _name not in ("fin", "fin2"):
        _a += len(quads_of(_groups))
NORM_GROUPS = dict(NORMS)


def al_before(name):
    if name == "xo":
        return AL0["lnffn"]
    return AL0[name] + (4 if name == "lnffn" else 0)


def tmp_at(first):
    return first if first < al_before("lnffn") else first - 4


HEADS = {"moba": 0, "na": 8, "mla": 16, "x": 24}


def block_program(nc, stream, ada, xT, memT, vecs, consts, onehot, relb, rpb, out, rel_dram,
                  rpb_dram, k_dram, v_dram, mh_dram, ml_dram):
    ctx = ExitStack()
    with ctx:
        def sb(name, shape, dt=F32):
            return ctx.enter_context(nc.sbuf_tensor(name, shape, dt))

        def sem(name):
            return ctx.enter_context(nc.semaphore(name))

        raw = sb("raw", [P, RAW, TILE])
        w_hi = sb("w_hi", [P, SLOTS, HALF], F32R)
        w_lo = sb("w_lo", [P, SLOTS, HALF], F32R)
        res = sb("res", [P, 16, S])
        a_hi = sb("a_hi", [P, 16, S], F32R)
        a_lo = sb("a_lo", [P, 16, S], F32R)
        arena = sb("arena", [P, 15 * 1024])
        work = sb("work", [P, 4096])
        rstd = sb("rstd", [P, 3 * S])
        vec = sb("vec", [P, NVEC])
        con = sb("con", [P, NCONST])
        ones = sb("ones", [P, P])
        mod = sb("mod", [P, 6, 16])
        small = sb("small", [P, 64])
        stage_v = sb("stage_v", [P, 1024])
        dts = sb("dts", [P, 12, 32])

        def region(r, chunks=8, at=0):
            a = r * 2048 + at * S
            return arena[:, a:a + chunks * S].rearrange("p (c t) -> p c t", t=S)

        hidden = arena[:, 0:FC * S].rearrange("p (c t) -> p c t", t=S)
        ada_acc = arena[:, 11264:13312]
        ada_ring = arena[:, 13312:15360].rearrange("p (s n) -> p s n", s=2)
        q_r, k_r = region(0), region(1)
        v_r = arena[:, 4096:6144].rearrange("p (t n) -> p t n", t=2)
        xs_r, z_r, bc_r = region(3), region(4), region(5, 4)
        xtok = arena[:, 2048:4096].rearrange("p (t n) -> p t n", t=2)
        ckv_r, qn_r, kn_r = region(3), region(4), region(5)
        v2_r = arena[:, 12288:14336].rearrange("p (t n) -> p t n", t=2)
        qx_r, kx_r = region(0, 16), region(2, 16)
        vx_r = arena[:, 8192:12288].rearrange("p (t n) -> p t n", t=2)

        tab_hot, tab_rel = arena[0:32, 6144:6656], arena[0:32, 6656:6664]
        tab_row, tab_rpb = arena[0:8, 6784:6784 + REL], arena[0:56, 7296:7296 + P]

        sq = work[:, 0:2048].rearrange("p (r n) -> p r n", r=2)
        tmp = work[:, 2048:4096].rearrange("p (r n) -> p r n", r=2)
        bias = work[:, 0:1024].rearrange("p (r n) -> p r n", r=2)
        logit = work[:, 1024:2048].rearrange("p (r n) -> p r n", r=2)
        prob = work[:, 2048:3072].rearrange("p (r n) -> p r n", r=2)
        probT = work[:, 3072:4096].rearrange("p (r n) -> p r n", r=2)
        conv = work[:, 0:2048].rearrange("p (r c t) -> p r c t", r=2, t=S)
        decay = work[:, 0:768].rearrange("p (r n) -> p r n", r=2)
        mix_m = work[:, 768:1536].rearrange("p (r n) -> p r n", r=2)
        seg_in = work[:, 1536:2304].rearrange("p (r n) -> p r n", r=2)
        gram = work[:, 2304:3072].rearrange("p (g n) -> p g n", g=2)

        ps = ctx.enter_context(nc.psum_tensor("ps", [P, 8, 512], F32))

        s_const, s_vec, s_res = sem("s_const"), sem("s_vec"), sem("s_res")
        s_mem = [sem(f"s_mem{q}") for q in range(4)]
        raw_landed = [sem(f"raw_landed{i}") for i in range(RAW)]
        ada_landed = [sem(f"ada_landed{i}") for i in range(4)]
        hi_ready, lo_ready = sem("hi_ready"), sem("lo_ready")
        half_used = sem("half_used")
        evac = [sem("evac0"), sem("evac1")]
        evac_b = sem("evac_b")
        ones_ready = sem("ones_ready")
        ada_used, ada_summed, mod_ready = sem("ada_used"), sem("ada_summed"), sem("mod_ready")
        dve_step = sem("dve_step")
        sq_ready, sq_used, sum_done = sem("sq_ready"), sem("sq_used"), sem("sum_done")
        tmp_ready, ah_ready, al_ready = sem("tmp_ready"), sem("ah_ready"), sem("al_ready")
        res_ready = sem("res_ready")
        hid_ready, hs_ready, hl_ready = sem("hid_ready"), sem("hs_ready"), sem("hl_ready")
        silu_ready = sem("silu_ready")
        scr_stored, rel_landed = sem("scr_stored"), sem("rel_landed")
        rel_ps, rel_row = sem("rel_ps"), sem("rel_row")
        rpb_zero, rpb_in = sem("rpb_zero"), sem("rpb_in")
        bias_landed = [sem("bias_landed0"), sem("bias_landed1")]
        spill = [sem("spill0"), sem("spill1")]
        spill_v, reload_done = sem("spill_v"), sem("reload_done")
        mem_stored, mem_back = sem("mem_stored"), sem("mem_back")
        s_ready, max_ready, exp_done, p_ready = (sem("s_ready"), sem("max_ready"),
                                                 sem("exp_done"), sem("p_ready"))
        pt_ready, pt_copied, o_ready, o_evac = (sem("pt_ready"), sem("pt_copied"),
                                                sem("o_ready"), sem("o_evac"))
        c_ready = sem("c_ready")
        dt_exp, dt_done = sem("dt_exp"), sem("dt_done")
        xt_ready, xt_copied, gram_ready, gram_masked = (sem("xt_ready"), sem("xt_copied"),
                                                        sem("gram_ready"), sem("gram_masked"))
        seg_ready, seg_summed, decay_ready, m_ready, y_ready, y_done = (
            sem("seg_ready"), sem("seg_summed"), sem("decay_ready"), sem("m_ready"),
            sem("y_ready"), sem("y_done"))
        rot_ready, rot_done = sem("rot_ready"), sem("rot_done")
        out_ready, s_out = sem("out_ready"), sem("s_out")

        def col(name, i=0, n=1):
            return vec[:, V0[name] + i:V0[name] + i + n]

        def const(name, a=0, b=None):
            width = dict(CONST)[name]
            return con[:, C0[name] + a:C0[name] + (width if b is None else b)]

        def acc(G):
            return ps[:, 2 * (G % 2):2 * (G % 2) + 2, :].rearrange("p b (c t) -> p (b c) t", t=S)

        def acc_tok(G):
            return ps[:, 2 * (G % 2):2 * (G % 2) + 2, :]

        def acc_b(c):
            return ps[:, 4 + 2 * c:6 + 2 * c, :].rearrange("p b (c t) -> p (b c) t", t=S)

        def ada_slot(i):
            if i < 2:
                return ada_ring[:, i]
            return arena[:, 8192 + 1024 * (i - 2):8192 + 1024 * (i - 1)]

        def xv_halves(h):
            return (12 + 2 * h, 13 + 2 * h) if h < 4 else (16 + h,)

        def head_out(u, chunks):
            if chunks == 1:
                return ps[:, 6 + u % 2:7 + u % 2, 0:S]
            return acc(u)[:, 0:chunks, :]

        def head_state(c):
            return ps[:, 4 + c % 2, 0:S]

        block = ctx.enter_context(nc.Block())

        @block.sync
        def _(sp):
            def stream_tile(t, slot, first=False):
                if not first:
                    sp.wait_ge(lo_ready, t * 2 - 2 * RAW + 2)
                sp.dma_start(raw[:, slot], stream[t]).then_inc(raw_landed[slot], 16)

            def ada_rows(u, pair, first=False, early=False):
                ring = 4 if early else 2
                for i in (2 * pair, 2 * pair + 1):
                    if not (first and i < ring):
                        sp.wait_ge(ada_used, u * 8 + (i + 1 - ring))
                    sp.dma_start(ada_slot(i % ring), ada[u * 8 + i]).then_inc(ada_landed[i % ring], 16)

            for q in range(4):
                sp.dma_start(region(0, 16)[:, 4 * q:4 * q + 4, :], memT[:, 4 * q:4 * q + 4, :])\
                  .then_inc(s_mem[q], 16)
                if q == 1:
                    sp.dma_start(vec[:, :], vecs).then_inc(s_vec, 16)
            for t in range(4):
                stream_tile(t, t, True)
            sp.dma_start(res[:, :, :], xT).then_inc(s_res, 16)
            for u in range(2):
                for pair in range(4):
                    ada_rows(u, pair, u == 0, True)
            with sp.Fori(1, 4) as g:
                for s in range(4):
                    stream_tile(g * 4 + s, s)
                    for pair in range(2):
                        ada_rows(g * 2 + s // 2, 2 * (s % 2) + pair, early=True)
            with sp.Fori(4, 12) as g:
                for s in range(4):
                    stream_tile(g * 4 + s, s)
                    ada_rows(g + 4, s)
            for t in range(48, 61):
                stream_tile(t, t % 4)
            with sp.Fori(0, 4) as g:
                for s in range(4):
                    stream_tile(g * 4 + (61 + s), (61 + s) % 4)
            with sp.Fori(0, 4) as g:
                for s in range(4):
                    stream_tile(g * 4 + (77 + s), (77 + s) % 4)
                    ada_rows(g + 16, s)
            for t in range(93, 101):
                stream_tile(t, t % 4)
            with sp.Fori(0, 8) as g:
                for s in range(8):
                    stream_tile(g * 8 + (101 + s), (101 + s) % 4)
                    if s % 2 == 0:
                        n = g * 4 + (160 + s // 2)
                        sp.wait_ge(ada_used, n - 1)
                        sp.dma_start(ada_slot(s // 2 % 2), ada[n]).then_inc(ada_landed[s // 2 % 2], 16)
            turns = (TILES - 165) // 4
            with sp.Fori(0, turns) as g:
                for s in range(4):
                    stream_tile(g * 4 + (165 + s), (165 + s) % 4)
            for t in range(165 + 4 * turns, TILES):
                stream_tile(t, t % 4)
            for q in range(4):
                sp.wait_ge(out_ready, q + 1)
                sp.dma_start(out[:, 4 * q:4 * q + 4, :], res[:, 4 * q:4 * q + 4, :]).then_inc(s_out, 16)
            sp.wait_ge(s_out, 64)

        @block.gpsimd
        def _(pool):
            pool.memset(ones[:, :], 1.0).then_inc(ones_ready, 1)

            def low_part(h, slot, tile_slot, part):
                pool.wait_ge(hi_ready, h + 1)
                pool.tensor_tensor(w_lo[:, slot], raw[:, tile_slot, part * HALF:(part + 1) * HALF],
                                   w_hi[:, slot].bitcast(F32), ALU.subtract).then_inc(lo_ready, 1)

            with pool.Fori(0, TILES // 4) as i:
                for s in range(8):
                    low_part(i * 8 + s, s % 4, s // 2, s % 2)
            for t in range(TILES // 4 * 4, TILES):
                for part in range(2):
                    low_part(2 * t + part, (2 * t + part) % 4, t % 4, part)

        @block.scalar
        def _(act):
            def hi(h, base):
                n = base if h is None else h + base
                tile_slot = (base // 2) % 4
                count = 16 * (base // 8 + 1)
                act.wait_ge(raw_landed[tile_slot], count if h is None else h * 2 + count)
                if h is not None or base >= SLOTS:
                    act.wait_ge(half_used, n - SLOTS + 1)
                act.copy(w_hi[:, base % 4],
                         raw[:, tile_slot, (base % 2) * HALF:(base % 2 + 1) * HALF]).then_inc(hi_ready, 1)

            def his(base, n, h=None):
                for i in range(n):
                    hi(h, base + i)

            def squares(name, source, ready):
                for q, (_, c, n, _, _) in enumerate(quads_of(NORM_GROUPS[name])):
                    ready(q)
                    k = SQ0[name] + q
                    if k >= 2:
                        act.wait_ge(sq_used, k - 1)
                    act.activation(sq[:, k % 2, 0:n * S].rearrange("p (c t) -> p c t", t=S), source(c, n),
                                   ACT.Square).then_inc(sq_ready, 1)

            def split_high(first, chunks, halves_before, source=None):
                if halves_before:
                    act.wait_ge(half_used, halves_before)
                for q, (c, n) in enumerate(chunks):
                    k = first + q
                    if source is None:
                        act.wait_ge(tmp_ready, tmp_at(first) + q + 1)
                        src = tmp[:, (tmp_at(first) + q) % 2, 0:n * S].rearrange("p (c t) -> p c t", t=S)
                    else:
                        src = source(c, n)
                    act.copy(a_hi[:, c:c + n, :], src).then_inc(ah_ready, 1)

            def norm(name, source, ready, halves_before):
                squares(name, source, ready)
                if name not in ("fin", "fin2"):
                    split_high(al_before(name), [(c, n) for _, c, n, _, _ in quads_of(NORM_GROUPS[name])],
                               halves_before)

            def evac_copy(G, dst):
                act.copy(dst, acc(G)).then_inc(evac[G % 2], 1)

            def group_done(halves):
                act.wait_ge(half_used, halves)

            act.dma_start(con[:, :], consts).then_inc(s_const, 16)
            act.dma_start(tab_hot, onehot).then_inc(rel_landed, 16)
            act.dma_start(tab_rel, relb).then_inc(rel_landed, 16)
            act.wait_ge(rpb_zero, 1)
            act.dma_start(tab_rpb[:, 48:79], rpb).then_inc(rpb_in, 16)

            act.wait_ge(s_vec, 16)
            act.activation(small[:, 16:32], col("c", 0, 16), ACT.Silu).then_inc(c_ready, 1)

            his(0, 4)
            squares("mem", lambda c, n: region(0, 16)[:, c:c + n, :], lambda q: act.wait_ge(s_mem[q], 16))
            act.wait_ge(rel_row, 1)
            act.dma_start(rel_dram, tab_row.unsqueeze(1).broadcast_to([8, P, REL])).then_inc(scr_stored, 16)
            act.wait_ge(rpb_in, 16)
            act.dma_start(rpb_dram, tab_rpb[:, 0:NA_W].unsqueeze(1).broadcast_to([56, GRID, NA_W])).then_inc(scr_stored, 16)
            split_high(0, [(c, n) for _, c, n, _, _ in quads_of(NORM_GROUPS["mem"])], 0)
            his(4, 4)
            act.wait_ge(al_ready, 4)
            act.dma_start(mh_dram, a_hi[:, :, :].bitcast(F32)).then_inc(mem_stored, 16)
            act.dma_start(ml_dram, a_lo[:, :, :].bitcast(F32)).then_inc(mem_stored, 16)
            act.wait_ge(s_res, 16)
            squares("mix", lambda c, n: res[:, c:c + n, :], lambda q: None)

            stage = [arena[:, 4096:5120], arena[:, 5120:6144]]

            def spill_group(G, dst):
                if G >= 2:
                    act.wait_ge(spill[G % 2], 16 * (G // 2))
                act.copy(stage[G % 2], acc_tok(G).rearrange("p b n -> p (b n)")).then_inc(evac[G % 2], 1)
                act.wait_ge(evac[G % 2], G // 2 + 1)
                act.dma_start(dst, stage[G % 2]).then_inc(spill[G % 2], 16)

            for G in range(1, 4):
                his(8 * G, 4)
                group_done(8 * G)
                spill_group(G - 1, k_dram[G - 1])
                his(8 * G + 4, 4)

            his(H0["win"], 4)
            group_done(H0["win"])
            spill_group(3, k_dram[3])
            act.wait_ge(mem_stored, 32)
            split_high(al_before("mix"), [(c, n) for _, c, n, _, _ in quads_of(NORM_GROUPS["mix"])],
                       H0["win"])
            his(H0["win"] + 4, 4)
            act.wait_ge(scr_stored, 32)
            act.wait_ge(spill[0], 32)
            act.wait_ge(spill[1], 32)
            for g in range(1, 12):
                last = g == 11
                his(H0["win"] + 8 * g, 2 if last else 4)
                group_done(H0["win"] + 8 * g)
                G = G0["win"] + g - 1
                if g - 1 < 4:
                    if g == 1:
                        act.wait_ge(tmp_ready, 4)
                    evac_copy(G, region(0, 16)[:, 4 * (g - 1):4 * g, :])
                elif g - 1 < 6:
                    j = g - 1 - 4
                    act.copy(v_r[:, :, 512 * j:512 * j + 512], acc_tok(G)).then_inc(evac[G % 2], 1)
                elif g - 1 in (6, 7):
                    j = g - 1 - 6
                    act.wait_ge(evac[G % 2], G // 2 + 1)
                    act.activation(xs_r[:, 4 * j:4 * j + 4, :], conv[:, j % 2], ACT.Silu).then_inc(silu_ready, 1)
                elif g - 1 in (8, 9):
                    j = g - 1 - 8
                    act.activation(z_r[:, 4 * j:4 * j + 4, :], acc(G), ACT.Silu).then_inc(evac[G % 2], 1)
                else:
                    act.wait_ge(evac[G % 2], G // 2 + 1)
                    act.activation(bc_r[:, :, :], conv[:, 0], ACT.Silu).then_inc(silu_ready, 1)
                if not last:
                    his(H0["win"] + 8 * g + 4, 4)
            his(H0["xv"], 4)

            def xv_group_out(j):
                G = G0["xv"] + j
                group_done(H0["xv"] + 8 * j + 8)
                if j:
                    act.wait_ge(spill_v, 16 * j)
                act.copy(stage_v[:, :], acc_tok(G).rearrange("p b n -> p (b n)")).then_inc(evac[G % 2], 1)
                act.wait_ge(evac[G % 2], G // 2 + 1)
                act.dma_start(v_dram[j], stage_v[:, :]).then_inc(spill_v, 16)

            def xv_step(n):
                if n >= 9 and n % 8 == 1:
                    xv_group_out(n // 8 - 1)
                hi(None, H0["xv"] + n + 4)

            def load_bias(u, kind, h):
                slot = bias[:, u % 2, :]
                if kind == "moba":
                    for qt in range(2):
                        src = bass.AP(rel_dram.tensor, h * P * REL + S - 1 - P * qt, [[REL - 1, P], [1, S]])
                        act.dma_start(slot[:, qt * S:(qt + 1) * S], src).then_inc(bias_landed[u % 2], 16)
                else:
                    for qt in range(2):
                        for a in range(2):
                            off = (7 * h + 3 - 2 * qt - a) * GRID * NA_W + GRID - 1
                            src = bass.AP(rpb_dram.tensor, off,
                                          [[NA_W - 1, GRID], [GRID * NA_W, 4], [1, GRID]])
                            dst = slot[a * GRID:(a + 1) * GRID, qt * S:(qt + 1) * S]
                            act.dma_start(dst.rearrange("p (r c) -> p r c", c=GRID), src)\
                               .then_inc(bias_landed[u % 2], 16)

            def attention(kind, dst, scale, chunks=1, beside=None):
                u0 = HEADS[kind]
                n = XH if kind == "x" else NH
                biased = kind in ("moba", "na")

                def exp(u):
                    act.wait_ge(max_ready, u + 1)
                    src = logit[:, u % 2, :] if biased else ps[:, 4 + u % 2, :]
                    for qt in range(2):
                        ins = act.activation(prob[:, u % 2, qt * S:(qt + 1) * S], src[:, qt * S:(qt + 1) * S],
                                             ACT.Exp, bias=small[:, 4 * (u % 2) + qt:4 * (u % 2) + qt + 1],
                                             scale=1.0 if biased else scale,
                                             accum_out=small[:, 8 + 4 * (u % 2) + qt:9 + 4 * (u % 2) + qt])
                    ins.then_inc(exp_done, 1)
                    if biased and u + 2 < u0 + n:
                        load_bias(u + 2, kind, u + 2 - u0)

                def copies(u):
                    act.wait_ge(pt_ready, u + 1)
                    act.copy(probT[:, u % 2, :], ps[:, 6 + u % 2, :]).then_inc(pt_copied, 1)

                def output(u):
                    act.wait_ge(o_ready, u + 1)
                    h = u - u0
                    act.copy(dst[:, h * chunks:(h + 1) * chunks, :], head_out(u, chunks)).then_inc(o_evac, 1)

                exp(u0)
                for u in range(u0, u0 + n):
                    if u + 1 < u0 + n:
                        exp(u + 1)
                    if beside is not None:
                        beside(2 * (u - u0))
                    copies(u)
                    if beside is not None:
                        beside(2 * (u - u0) + 1)
                    if u > u0:
                        output(u - 1)
                output(u0 + n - 1)

            act.wait_ge(silu_ready, 3)
            load_bias(0, "moba", 0)
            load_bias(1, "moba", 1)
            act.wait_ge(half_used, H0["xv"])
            act.dma_start(a_hi[:, :, :].bitcast(F32), mh_dram).then_inc(mem_back, 16)
            act.dma_start(a_lo[:, :, :].bitcast(F32), ml_dram).then_inc(mem_back, 16)
            attention("moba", q_r, HD ** -0.5, beside=lambda i: xv_step(i - 4) if i >= 4 else None)

            act.wait_ge(dt_done, 1)
            act.activation(dts[:, 2, :], dts[:, 1, :], ACT.Exp)
            act.activation(dts[:, 3, 0:16], col("alog", 0, 16), ACT.Exp).then_inc(dt_exp, 1)
            for tt in range(2):
                for hf in range(2):
                    act.wait_ge(xt_ready, 2 * tt + hf + 1)
                    act.copy(xtok[:, tt, hf * 512:(hf + 1) * 512], ps[:, 4 + 2 * tt + hf, :]).then_inc(xt_copied, 1)
            for h in range(STATE_HEADS):
                act.wait_ge(seg_summed, h + 1)
                if h >= 2:
                    act.wait_ge(m_ready, h - 1)
                act.activation(decay[:, h % 2, :], ps[:, 6 + h % 2, 0:384], ACT.Exp).then_inc(decay_ready, 1)
                for n in xv_halves(h):
                    xv_step(n)
            xv_group_out(3)

            def mixin_ready(q):
                act.wait_ge(y_done, 8)

            def mixin_source(c, n):
                return q_r[:, c:c + n, :] if c < 8 else z_r[:, c - 8:c - 8 + n, :]

            def residual_ready(name):
                def wait(q):
                    if name == "fin":
                        act.wait_ge(res_ready, q + 1)
                    elif name in ("down", "down2") and q >= 2:
                        act.wait_ge(evac_b, 2 * (name == "down2") + q - 1)
                    else:
                        G = G0[name] + q
                        act.wait_ge(evac[G % 2], G // 2 + 1)
                return wait

            norm("mixin", mixin_source, mixin_ready, H0["wout"])
            his(H0["wout"] + 4, 4)
            his(H0["wout"] + 8, 24)
            his(H0["up"], 4)
            norm("ffn", lambda c, n: res[:, c:c + n, :], residual_ready("wout"), H0["up"])
            his(H0["up"] + 4, 4)

            def ffn_silu(par, G, i=None):
                act.wait_ge(evac[G % 2], G // 2 + 1 if i is None else i + (G // 2 + 1))
                act.activation(conv[:, par, 0:2, :], conv[:, par, 0:2, :], ACT.Silu).then_inc(silu_ready, 1)

            his(H0["up"] + 8, 4)
            ffn_silu(0, G0["up"])
            his(H0["up"] + 12, 4)
            with act.Fori(0, 10) as i:
                for p in range(2):
                    his(H0["up"] + 16 + 8 * p, 4, h=i * 16)
                    ffn_silu((1 + p) % 2, G0["up"] + 1 + p, i)
                    his(H0["up"] + 20 + 8 * p, 4, h=i * 16)
            his(H0["down"], 2)
            ffn_silu(1, G0["up"] + 21)
            his(H0["down"] + 2, 2)

            def hidden_high(n):
                quad, a = n % 11, (n % 2) * 4
                act.copy(a_hi[:, a:a + 4, :], hidden[:, 4 * quad:4 * quad + 4, :]).then_inc(hs_ready, 1)

            def down(name):
                base = H0[name]
                if name == "down":
                    act.wait_ge(hid_ready, 22)
                else:
                    for G in (G0["gu"] + 20, G0["gu"] + 21):
                        act.wait_ge(evac[G % 2], G // 2 + 1)
                act.wait_ge(half_used, base)
                hidden_high(0)
                hidden_high(1)
                his(base + 4, 4)
                for n in range(2, 22):
                    act.wait_ge(half_used, base + 4 * (n - 1))
                    hidden_high(n)
                    his(base + 4 * n, 4)

            down("down")

            his(H0["win2"], 4)
            norm("fin", lambda c, n: res[:, c:c + n, :], residual_ready("down"), 0)
            norm("lnmix", lambda c, n: res[:, c:c + n, :], residual_ready("fin"), H0["win2"])
            his(H0["win2"] + 4, 4)
            for g in range(1, 7):
                his(H0["win2"] + 8 * g, 4)
                group_done(H0["win2"] + 8 * g)
                G = G0["win2"] + g - 1
                if g - 1 < 4:
                    evac_copy(G, region(0, 16)[:, 4 * (g - 1):4 * g, :])
                else:
                    j = g - 1 - 4
                    act.copy(v_r[:, :, 512 * j:512 * j + 512], acc_tok(G)).then_inc(evac[G % 2], 1)
                if g < 6:
                    his(H0["win2"] + 8 * g + 4, 4)

            def win2_step(n):
                if n == 9:
                    group_done(H0["win2"] + 56)
                    evac_copy(G0["win2"] + 6, ckv_r[:, 0:4, :])
                hi(None, H0["win2"] + 48 + n + 4)

            act.wait_ge(al_ready, al_before("lnmix") + 4)
            load_bias(8, "na", 0)
            load_bias(9, "na", 1)
            attention("na", q_r, HD ** -0.5, beside=win2_step)
            G = G0["win2"] + 7
            group_done(H0["win2"] + 64)
            act.copy(ckv_r[:, 4:7, :], acc(G)[:, 0:3, :]).then_inc(evac[G % 2], 1)
            act.wait_ge(exp_done, 16)
            act.wait_ge(pt_copied, 16)
            act.wait_ge(o_evac, 16)

            def ckv_ready(q):
                G = G0["win2"] + 6 + q
                act.wait_ge(evac[G % 2], G // 2 + 1)

            norm("qkv", lambda c, n: ckv_r[:, c:c + n, :], ckv_ready, H0["uq"])
            lat = H0["uq"]
            dsts = [(2, qn_r[:, 0:4, :]), (4, qn_r[:, 4:8, :]), (6, ckv_r[:, 0:4, :]),
                    (7, kn_r[:, 0:4, :]), (8, kn_r[:, 4:8, :]), (9, 0), (10, 1)]
            issued = 4
            for i, (used, dst) in enumerate(dsts):
                want = min(used + 3, 14)
                if want > issued:
                    his(lat + issued, want - issued)
                    issued = want
                group_done(lat + used)
                G = G0["uq"] + i
                if isinstance(dst, int):
                    act.copy(v2_r[:, :, 512 * dst:512 * dst + 512], acc_tok(G)).then_inc(evac[G % 2], 1)
                else:
                    if i == 2:
                        act.wait_ge(tmp_ready, tmp_at(al_before("qkv")) + 2)
                    act.copy(dst, acc(G)).then_inc(evac[G % 2], 1)
            if issued < 14:
                his(lat + issued, 14 - issued)

            act.wait_ge(al_ready, al_before("qkv") + 2)
            attention("mla", qn_r, 192 ** -0.5)

            def mixin2_source(c, n):
                return q_r[:, c:c + n, :] if c < 8 else qn_r[:, c - 8:c - 8 + n, :]

            norm("mixin2", mixin2_source, lambda q: act.wait_ge(o_evac, 16 if q < 2 else 24), H0["wout2"])
            act.wait_ge(al_ready, al_before("mixin2") + 4)
            act.wait_ge(spill_v, 64)
            for j in range(4):
                act.dma_start(kx_r[:, 4 * j:4 * j + 4, :], k_dram[j].rearrange("p (c t) -> p c t", t=S))\
                   .then_inc(reload_done, 16)
                act.dma_start(vx_r[:, :, 512 * j:512 * j + 512], v_dram[j].rearrange("p (t n) -> p t n", t=2))\
                   .then_inc(reload_done, 16)
            his(H0["wout2"] + 4, 28)
            his(H0["xq"], 4)
            norm("lnmem", lambda c, n: res[:, c:c + n, :], residual_ready("wout2"), H0["xq"])
            his(H0["xq"] + 4, 4)
            for g in range(1, 5):
                if g < 4:
                    his(H0["xq"] + 8 * g, 4)
                else:
                    his(H0["xo"], 4)
                group_done(H0["xq"] + 8 * g)
                evac_copy(G0["xq"] + g - 1, qx_r[:, 4 * (g - 1):4 * g, :])
                if g < 4:
                    his(H0["xq"] + 8 * g + 4, 4)
            attention("x", qx_r, 512 ** -0.5, chunks=4)
            act.wait_ge(half_used, H0["xo"])
            for q in range(4):
                act.wait_ge(o_evac, 25 + q)
                act.copy(a_hi[:, 4 * q:4 * q + 4, :], qx_r[:, 4 * q:4 * q + 4, :]).then_inc(ah_ready, 1)
            his(H0["xo"] + 4, 28)
            his(H0["gu"], 4)
            norm("lnffn", lambda c, n: res[:, c:c + n, :], residual_ready("xo"), H0["gu"])
            his(H0["gu"] + 4, 4)

            def gate_silu(par, G_par, used, used_prev):
                act.wait_ge(half_used, used)
                if used_prev is not None:
                    act.wait_ge(evac[G_par % 2], used_prev)
                act.activation(conv[:, par, 0:2, :], acc(G_par)[:, 0:2, :], ACT.Silu).then_inc(silu_ready, 1)

            gb = H0["gu"]
            his(gb + 8, 4)
            gate_silu(0, G0["gu"], gb + 8, None)
            his(gb + 12, 4)
            with act.Fori(0, 10) as i:
                for p in range(2):
                    his(gb + 16 + 8 * p, 4, h=i * 16)
                    gate_silu((1 + p) % 2, G0["gu"] + 1 + p, i * 16 + (gb + 16 + 8 * p),
                              i + (G0["gu"] + 1 + p) // 2)
                    his(gb + 20 + 8 * p, 4, h=i * 16)
            his(H0["down2"], 2)
            gate_silu(1, G0["gu"] + 21, gb + 8 * 22, (G0["gu"] + 21) // 2)
            his(H0["down2"] + 2, 2)
            down("down2")
            norm("fin2", lambda c, n: res[:, c:c + n, :], residual_ready("down2"), 0)

        @block.tensor
        def _(pe):
            def wait_half(n):
                pe.wait_ge(hi_ready, n)
                pe.wait_ge(lo_ready, n)

            def half_T(slot, out4, c0, first, last, chunks=4, inc=True):
                for k in range(2):
                    for f in range(chunks):
                        w = slice(k * 512 + f * P, k * 512 + (f + 1) * P)
                        o = out4[:, f, :]
                        pe.matmul(o, w_hi[:, slot, w], a_hi[:, c0 + k, :], start=first and k == 0 and f % 2 == 0,
                                  stop=False, skip_group_check=True)
                        pe.matmul(o, w_hi[:, slot, w], a_lo[:, c0 + k, :], start=False, stop=False,
                                  skip_group_check=True)
                        mm = pe.matmul(o, w_lo[:, slot, w], a_hi[:, c0 + k, :], start=False,
                                       stop=last and k == 1, skip_group_check=True)
                mm.then_inc(half_used, 1)

            def half_N(slot, out2, c0, first, last, width=512):
                for k in range(2):
                    for t in range(2):
                        w = slice(k * 512, k * 512 + width)
                        a = slice(t * P, (t + 1) * P)
                        pe.matmul(out2[:, t, 0:width], a_hi[:, c0 + k, a], w_hi[:, slot, w],
                                  start=first and k == 0, stop=False, skip_group_check=True)
                        pe.matmul(out2[:, t, 0:width], a_lo[:, c0 + k, a], w_hi[:, slot, w],
                                  start=False, stop=False, skip_group_check=True)
                        mm = pe.matmul(out2[:, t, 0:width], a_hi[:, c0 + k, a], w_lo[:, slot, w],
                                       start=False, stop=last and k == 1, skip_group_check=True)
                mm.then_inc(half_used, 1)

            def al_quad(k):
                pe.wait_ge(al_ready, k)

            def group(kind, G, h0, al=None, i=None, chunks=4):
                n = G // 2
                pe.wait_ge(evac[G % 2], n if i is None else i + n) if (i is not None or n) else None
                for s in range(8):
                    wait_half(h0 + s + 1 if i is None else i * 16 + (h0 + s + 1))
                    if al is not None and s % 2 == 0:
                        al_quad(al + s // 2 + 1)
                    if kind == "T":
                        half_T((h0 + s) % 4, acc(G), 2 * s, s == 0, s == 7, chunks)
                    else:
                        half_N((h0 + s) % 4, acc_tok(G), 2 * s, s == 0, s == 7)

            def groups(kind, name, a, b, al=None):
                G, h = G0[name], H0[name]
                if al is not None:
                    group(kind, G + a, h + 8 * a, al)
                    a += 1
                if (b - a) // 2 >= 2:
                    n = (b - a) // 2
                    with pe.Fori(0, n) as i:
                        group(kind, G + a, h + 8 * a, i=i)
                        group(kind, G + a + 1, h + 8 * a + 8, i=i)
                    a += 2 * n
                for g in range(a, b):
                    group(kind, G + g, h + 8 * g)

            def sums(name):
                for q, (g, _, n, start, stop) in enumerate(quads_of(NORM_GROUPS[name])):
                    k = SQ0[name] + q
                    pe.wait_ge(sq_ready, k + 1)
                    for j in range(n):
                        mm = pe.matmul(ps[:, 4 + g // 2, (g % 2) * S:(g % 2) * S + S], ones[:, :],
                                       sq[:, k % 2, j * S:(j + 1) * S], start=start and j == 0,
                                       stop=stop and j == n - 1, skip_group_check=True)
                    mm.then_inc(sq_used, 1)

            def ada_sum(s):
                pe.wait_ge(ada_used, 32 * (s + 1))
                if s:
                    pe.wait_ge(mod_ready, s)
                for c in range(16):
                    mm = pe.matmul(ps[:, 7, c:c + 1], ada_acc[:, c * P:(c + 1) * P], ones[:, 0:1],
                                   start=True, stop=True, skip_group_check=True)
                mm.then_inc(ada_summed, 1)

            ident = const("ident")
            pe.wait_ge(ones_ready, 1)
            pe.wait_ge(s_const, 16)
            pe.wait_ge(rel_landed, 32)
            pe.matmul(ps[0:8, 5, 0:S], tab_rel, tab_hot[:, 0:S],
                      start=True, stop=True).then_inc(rel_ps, 1)
            sums("mem")
            groups("T", "xk", 0, 1, al=0)
            sums("mix")
            groups("T", "xk", 1, 2)
            ada_sum(0)
            groups("T", "xk", 2, 4)
            ada_sum(1)
            groups("T", "win", 0, 4, al=al_before("mix"))
            ada_sum(2)
            groups("N", "win", 4, 6)
            groups("T", "win", 6, 8)
            ada_sum(3)
            groups("T", "win", 8, 11)
            G, h = G0["dt"], H0["dt"]
            pe.wait_ge(evac[G % 2], G // 2)
            wait_half(h + 2)
            for t in range(2):
                for k in range(16):
                    a = slice(t * P, (t + 1) * P)
                    w = slice(k * 16, (k + 1) * 16)
                    o = acc_tok(G)[:, t, 0:16]
                    pe.matmul(o, a_hi[:, k, a], w_hi[:, h % 4, w], start=k == 0, stop=False,
                              skip_group_check=True)
                    pe.matmul(o, a_lo[:, k, a], w_hi[:, h % 4, w], start=False, stop=False,
                              skip_group_check=True)
                    mm = pe.matmul(o, a_hi[:, k, a], w_lo[:, h % 4, w], start=False, stop=k == 15,
                                   skip_group_check=True)
            mm.then_inc(half_used, 2)

            def attention(kind, q_of, k_of, v, chunks=1, rope=None, beside=None):
                u0 = HEADS[kind]
                n = XH if kind == "x" else NH

                def scores(u):
                    h = u - u0
                    if u >= 2:
                        pe.wait_ge(exp_done, u - 1)
                    for qt in range(2):
                        o = ps[:, 4 + u % 2, qt * S:(qt + 1) * S]
                        a = slice(qt * P, (qt + 1) * P)
                        for c in range(chunks):
                            mm = pe.matmul(o, q_of(h, c)[:, a], k_of(h, c), start=c == 0,
                                           stop=c == chunks - 1 and rope is None, skip_group_check=True)
                        if rope is not None:
                            lo, qr, kr = rope(h)
                            mm = pe.matmul(o, qr[lo:lo + 64, a], kr[lo:lo + 64, :], start=False, stop=True,
                                           skip_group_check=True)
                    mm.then_inc(s_ready, 1)

                def turn(u):
                    pe.wait_ge(p_ready, u + 1)
                    if u >= 2:
                        pe.wait_ge(pt_copied, u - 1)
                        pe.wait_ge(o_evac, u - 1)
                    for kt in range(2):
                        for qt in range(2):
                            mm = pe.transpose(ps[:, 6 + u % 2, kt * S + qt * P:kt * S + (qt + 1) * P],
                                              prob[:, u % 2, qt * S + kt * P:qt * S + (kt + 1) * P], ident)
                    mm.then_inc(pt_ready, 1)

                def values(u):
                    h = u - u0
                    pe.wait_ge(pt_copied, u + 1)
                    for c in range(chunks):
                        o = head_out(u, chunks)[:, c, :]
                        for kt in range(2):
                            w = slice((h * chunks + c) * P, (h * chunks + c + 1) * P)
                            mm = pe.matmul(o, v[:, kt, w], probT[:, u % 2, kt * S:(kt + 1) * S],
                                           start=kt == 0, stop=kt == 1, skip_group_check=True)
                    mm.then_inc(o_ready, 1)

                scores(u0)
                for u in range(u0, u0 + n):
                    if u + 1 < u0 + n:
                        scores(u + 1)
                    if beside is not None:
                        beside(2 * (u - u0))
                    turn(u)
                    if beside is not None:
                        beside(2 * (u - u0) + 1)
                    if u > u0:
                        values(u - 1)
                values(u0 + n - 1)

            for g in range(4, 6):
                G = G0["win"] + g
                pe.wait_ge(evac[G % 2], G // 2 + 1)

            def xv_half(n):
                G, s = G0["xv"] + n // 8, n % 8
                if s == 0:
                    pe.wait_ge(evac[G % 2], G // 2)
                if n == 0:
                    pe.wait_ge(mem_back, 32)
                wait_half(H0["xv"] + n + 1)
                half_N((H0["xv"] + n) % 4, acc_tok(G), 2 * s, s == 0, s == 7)

            attention("moba", lambda h, c: q_r[:, h, :], lambda h, c: k_r[:, h, :], v_r,
                      beside=lambda i: xv_half(i - 4) if i >= 4 else None)

            pe.wait_ge(silu_ready, 3)
            pe.wait_ge(exp_done, 8)
            pe.wait_ge(o_evac, 8)
            for t in range(2):
                for hf in range(2):
                    for c in range(4):
                        mm = pe.transpose(ps[:, 4 + 2 * t + hf, c * P:(c + 1) * P],
                                          xs_r[:, 4 * hf + c, t * P:(t + 1) * P], ident)
                    mm.then_inc(xt_ready, 1)
            pe.wait_ge(xt_copied, 2)
            for g in range(2):
                pe.matmul(ps[:, 4 + g, 0:S], bc_r[:, g, 0:P], bc_r[:, 2 + g, :], start=True, stop=True,
                          skip_group_check=True)
                pe.matmul(ps[:, 4 + g, S:S + P], bc_r[:, g, P:S], bc_r[:, 2 + g, P:S], start=True,
                          stop=True, skip_group_check=True).then_inc(gram_ready, 1)
            tri, after = const("tri"), const("after")

            def segment(h):
                pe.wait_ge(seg_ready, h + 1)
                if h >= 2:
                    pe.wait_ge(decay_ready, h - 1)
                else:
                    pe.wait_ge(xt_copied, 3 + h)
                o = ps[:, 6 + h % 2, :]
                r = seg_in[:, h % 2, :]
                pe.matmul(o[:, 0:S], after, r[:, 0:S], start=True, stop=False, skip_group_check=True)
                pe.matmul(o[:, P:S], ones[:, :], r[:, S:S + P], start=False, stop=True,
                          skip_group_check=True)
                pe.matmul(o[:, S:S + P], after, r[:, S:S + P], start=True, stop=True,
                          skip_group_check=True).then_inc(seg_summed, 1)

            def state_out(h):
                pe.wait_ge(m_ready, h + 1)
                c, lo = h // 2, 64 * (h % 2)
                if h == 0:
                    pe.wait_ge(xt_copied, 4)
                if h % 2 == 0 and c >= 2:
                    pe.wait_ge(y_done, c - 1)
                o = head_state(c)[lo:lo + 64, :]
                w = slice(h * 64, (h + 1) * 64)
                m = mix_m[:, h % 2, :]
                pe.matmul(o, xtok[:, 0, w], m[:, 0:S], start=True, stop=False, skip_group_check=True)
                pe.matmul(o[:, P:S], xtok[:, 1, w], m[:, S:S + P], start=False, stop=True,
                          skip_group_check=True).then_inc(y_ready, 1)

            segment(0)
            for h in range(STATE_HEADS):
                if h + 1 < STATE_HEADS:
                    segment(h + 1)
                for n in xv_halves(h):
                    xv_half(n)
                state_out(h)

            sums("mixin")
            pe.wait_ge(y_done, 8)
            groups("T", "wout", 0, 4, al=al_before("mixin"))
            ada_sum(4)
            sums("ffn")
            groups("T", "up", 0, 22, al=al_before("ffn"))
            ada_sum(5)

            def down(name, hs0):
                G, base = G0[name], H0[name]
                outs = [[acc(G), acc(G + 1)], [acc_b(0), acc_b(1)]]
                sets = [G % 2, (G + 1) % 2]

                def step(half, n, i, first, last):
                    par = n % 2
                    base_n = base + 4 * n
                    pe.wait_ge(hl_ready, hs0 + n + 1 if i is None else i * 2 + (hs0 + n + 1))
                    for s in range(4):
                        cg, kp = s // 2, s % 2
                        if first and kp == 0 and half == 0:
                            pe.wait_ge(evac[sets[cg]], (G + cg) // 2)
                        if first and s == 0 and half == 1:
                            pe.wait_ge(mod_ready, len(ADA_ORDER))
                        wait_half(base_n + s + 1 if i is None else i * 8 + (base_n + s + 1))
                        half_T((base_n + s) % 4, outs[half][cg], par * 4 + 2 * kp, first and kp == 0,
                               last and kp == 1)

                for half in range(2):
                    n0 = 11 * half
                    step(half, n0, None, True, False)
                    with pe.Fori(0, 5) as i:
                        step(half, n0 + 1, i, False, False)
                        step(half, n0 + 2, i, False, False)

            down("down", 0)

            pe.wait_ge(evac_b, 2)
            sums("fin")
            sums("lnmix")

            groups("T", "win2", 0, 4, al=al_before("lnmix"))
            groups("N", "win2", 4, 6)

            def win2_half(n):
                g, s = 6 + n // 8, n % 8
                G = G0["win2"] + g
                if s == 0:
                    pe.wait_ge(evac[G % 2], G // 2)
                wait_half(H0["win2"] + 8 * g + s + 1)
                half_T((H0["win2"] + 8 * g + s) % 4, acc(G), 2 * s, s == 0, s == 7, 4 if g == 6 else 3)

            for g in range(4, 6):
                G = G0["win2"] + g
                pe.wait_ge(evac[G % 2], G // 2 + 1)
            attention("na", lambda h, c: q_r[:, h, :], lambda h, c: k_r[:, h, :], v_r, beside=win2_half)
            pe.wait_ge(exp_done, 16)
            sums("qkv")
            a0, lat = al_before("qkv"), H0["uq"]
            for g in range(3):
                G = G0["uq"] + g
                pe.wait_ge(evac[G % 2], G // 2)
                for s in range(2):
                    wait_half(lat + 2 * g + s + 1)
                    if g == 0:
                        al_quad(a0 + 1)
                    half_T((lat + 2 * g + s) % 4, acc(G), 2 * s, s == 0, s == 1)
            for g in range(4):
                G = G0["ukv"] + g
                pe.wait_ge(evac[G % 2], G // 2)
                wait_half(lat + 6 + g + 1)
                if g == 0:
                    al_quad(a0 + 2)
                if g < 2:
                    half_T((lat + 6 + g) % 4, acc(G), 4, True, True)
                else:
                    half_N((lat + 6 + g) % 4, acc_tok(G), 4, True, True)
            G = G0["ukv"] + 3
            pe.wait_ge(evac[G % 2], G // 2 + 1)
            pe.wait_ge(evac[(G + 1) % 2], (G + 1) // 2)
            for j, c in enumerate([0, 1, 2, 3, 6]):
                if j:
                    pe.wait_ge(rot_done, j)
                pe.matmul(ps[:, 5, 0:S], const("rot"), ckv_r[:, c, :], start=True, stop=True,
                          skip_group_check=True).then_inc(rot_ready, 1)
            pe.wait_ge(rot_done, 5)
            attention("mla", lambda h, c: qn_r[:, h, :], lambda h, c: kn_r[:, h, :], v2_r,
                      rope=lambda h: (64 * (h % 2), ckv_r[:, h // 2, :], ckv_r[:, 6, :]))
            sums("mixin2")
            pe.wait_ge(o_evac, 24)
            groups("T", "wout2", 0, 4, al=al_before("mixin2"))
            sums("lnmem")
            groups("T", "xq", 0, 4, al=al_before("lnmem"))
            for g in range(2, 4):
                G = G0["xq"] + g
                pe.wait_ge(evac[G % 2], G // 2 + 1)
            pe.wait_ge(reload_done, 128)
            attention("x", lambda h, c: qx_r[:, 4 * h + c, :], lambda h, c: kx_r[:, 4 * h + c, :], vx_r,
                      chunks=4)
            pe.wait_ge(o_evac, 28)
            groups("T", "xo", 0, 4, al=al_before("xo"))
            sums("lnffn")
            groups("T", "gu", 0, 22, al=al_before("lnffn"))
            down("down2", 22)
            pe.wait_ge(evac_b, 4)
            sums("fin2")

        @block.vector
        def _(dve):
            steps = [0]

            def link(ins):
                steps[0] += 1
                ins.then_inc(dve_step, 1)

            def settle(extra=None):
                dve.wait_ge(dve_step, steps[0] if extra is None else extra + steps[0])

            def chunked(ap):
                return ap.rearrange("p (c t) -> p c t", t=S)

            def ada_unit(u):
                s, k4 = u // 4, u % 4
                if k4 == 0 and s:
                    dve.wait_ge(ada_summed, s)
                for i in range(8):
                    n = 8 * u + i
                    ring = 4 if n < ADA_EARLY else 2
                    turn = n // 4 if n < ADA_EARLY else (ADA_EARLY // 4 + (n - ADA_EARLY) // 2)
                    dve.wait_ge(ada_landed[i % ring], 16 * (turn + 1))
                    k, part = 4 * k4 + i // 2, i % 2
                    a = ada_acc[:, part * 1024:(part + 1) * 1024]
                    ck = small[:, 16 + k:17 + k]
                    if k == 0:
                        ins = dve.tensor_scalar(a, ada_slot(i % ring), ck, None, ALU.mult)
                    else:
                        dve.wait_ge(ada_used, n - 1)
                        ins = dve.scalar_tensor_tensor(out=a, in0=ada_slot(i % ring), scalar=ck, in1=a,
                                                       op0=ALU.mult, op1=ALU.add)
                    ins.then_inc(ada_used, 1)

            def ada_mod(s):
                dve.wait_ge(ada_summed, s + 1)
                sl = ADA_ORDER[s]
                dve.tensor_tensor(mod[:, s, :], ps[:, 7, 0:16], col("b_ada", 16 * sl, 16), ALU.add)\
                   .then_inc(mod_ready, 1)
                dve.wait_ge(mod_ready, s + 1)
                if sl in (1, 4):
                    g = col("mix_g" if sl == 1 else "ffn_g", 0, 16)
                    link(dve.scalar_tensor_tensor(out=mod[:, s, :], in0=mod[:, s, :], scalar=1.0, in1=g,
                                                  op0=ALU.add, op1=ALU.mult))
                    settle()

            def newton(name):
                groups = NORM_GROUPS[name]
                dve.wait_ge(sq_used, SQ0[name] + len(quads_of(groups)))
                w = len(groups) * S
                v, u, y = work[:, 0:w], work[:, 768:768 + w], rstd[:, 0:w]
                for g, (_, width) in enumerate(groups):
                    link(dve.tensor_scalar(v[:, g * S:(g + 1) * S],
                                           ps[:, 4 + g // 2, (g % 2) * S:(g % 2) * S + S],
                                           1.0 / width, EPS,
                                           ALU.mult, ALU.add))
                settle()
                link(dve.tensor_scalar(u.bitcast(I32), v.bitcast(I32), 1, None, ALU.logical_shift_right))
                settle()
                link(dve.tensor_scalar(y.bitcast(I32), u.bitcast(I32), -1.0, float(0x5F3759DF), ALU.mult,
                                       ALU.add))
                settle()
                for _ in range(3):
                    link(dve.scalar_tensor_tensor(out=u, in0=y, scalar=-0.5, in1=v, op0=ALU.mult,
                                                  op1=ALU.mult))
                    settle()
                    link(dve.tensor_tensor(u, u, y, ALU.mult))
                    settle()
                    link(dve.scalar_tensor_tensor(out=y, in0=u, scalar=1.5, in1=y, op0=ALU.add,
                                                  op1=ALU.mult))
                    settle()

            def norm(name, source, gain, shift=None, summed=False):
                if not summed:
                    newton(name)
                first = al_before(name)
                t0 = tmp_at(first)
                quads = quads_of(NORM_GROUPS[name])

                def low(q):
                    _, c, n, _, _ = quads[q]
                    dve.wait_ge(ah_ready, first + q + 1)
                    dve.tensor_tensor(a_lo[:, c:c + n, :], chunked(tmp[:, (t0 + q) % 2, 0:n * S]),
                                      a_hi[:, c:c + n, :].bitcast(F32), ALU.subtract).then_inc(al_ready, 1)

                for q, (g, c, n, _, _) in enumerate(quads):
                    if first + q >= 2:
                        dve.wait_ge(al_ready, max(first + q - 1, first))
                    for j in range(n):
                        o = tmp[:, (t0 + q) % 2, j * S:(j + 1) * S]
                        ins = dve.scalar_tensor_tensor(out=o, in0=source(c + j), scalar=gain(c + j),
                                                       in1=rstd[:, g * S:(g + 1) * S], op0=ALU.mult,
                                                       op1=ALU.mult)
                        if shift is not None:
                            link(ins)
                    if shift is not None:
                        settle()
                        for j in range(n):
                            o = tmp[:, (t0 + q) % 2, j * S:(j + 1) * S]
                            ins = dve.tensor_scalar(o, o, shift(c + j), None, ALU.add)
                    ins.then_inc(tmp_ready, 1)
                    dve.wait_ge(tmp_ready, t0 + q + 1)
                    if q:
                        low(q - 1)
                low(len(quads) - 1)

            def norm_in_place(name, gain, signal):
                newton(name)
                for c in range(16):
                    ins = dve.scalar_tensor_tensor(out=res[:, c, :], in0=res[:, c, :], scalar=gain(c),
                                                   in1=rstd[:, 0:S], op0=ALU.mult, op1=ALU.mult)
                    if c % 4 == 3:
                        ins.then_inc(signal, 1)
                return signal

            def residual(q, src, halves, signal, gate=None):
                dve.wait_ge(half_used, halves)
                r = res[:, 4 * q:4 * q + 4, :]
                if gate is None:
                    ins = dve.tensor_tensor(r, src, r, ALU.add)
                else:
                    for j in range(4):
                        ins = dve.scalar_tensor_tensor(out=r[:, j, :], in0=src[:, j, :],
                                                       scalar=mod[:, gate, 4 * q + j:4 * q + j + 1],
                                                       in1=r[:, j, :], op0=ALU.mult, op1=ALU.add)
                ins.then_inc(signal, 1)

            def residual_groups(name, gate=None, between=None):
                for g in range(4):
                    if between is not None:
                        between(g)
                    G = G0[name] + g
                    residual(g, acc(G), H0[name] + 8 * g + 8, evac[G % 2], gate)

            def down(name, hs0, gate=None):
                for n in range(22):
                    dve.wait_ge(hs_ready, hs0 + n + 1)
                    quad, a = n % 11, (n % 2) * 4
                    dve.tensor_tensor(a_lo[:, a:a + 4, :], hidden[:, 4 * quad:4 * quad + 4, :],
                                      a_hi[:, a:a + 4, :].bitcast(F32), ALU.subtract).then_inc(hl_ready, 1)
                    if n == 12:
                        for c in range(2):
                            G = G0[name] + c
                            residual(c, acc(G), H0[name] + 44, evac[G % 2], gate)
                for c in range(2):
                    residual(2 + c, acc_b(c), H0[name] + 88, evac_b, gate)

            def convolve(dst, src, w, b, taps, signal, extra=None):
                for c in range(4):
                    link(dve.tensor_scalar(dst[:, c, :], src[:, c, :], w(c, taps - 1), b(c), ALU.mult,
                                           ALU.add))
                for shift in range(1, taps):
                    settle(extra)
                    for c in range(4):
                        ins = dve.scalar_tensor_tensor(out=dst[:, c, shift:S], in0=src[:, c, 0:S - shift],
                                                       scalar=w(c, taps - 1 - shift),
                                                       in1=dst[:, c, shift:S], op0=ALU.mult, op1=ALU.add)
                        if shift < taps - 1:
                            link(ins)
                ins.then_inc(signal, 1)

            def conv_ssm(g, j, par):
                G = G0["win"] + g
                dve.wait_ge(half_used, H0["win"] + 8 * g + 8)
                if j == 2:
                    dve.wait_ge(silu_ready, 1)
                convolve(conv[:, par], acc(G), lambda c, t: col("cs_w", 4 * (4 * j + c) + t),
                         lambda c: col("cs_b", 4 * j + c), 4, evac[G % 2])

            def attention(kind, scale):
                u0 = HEADS[kind]
                n = XH if kind == "x" else NH
                biased = kind in ("moba", "na")

                def front(u):
                    dve.wait_ge(s_ready, u + 1)
                    src = ps[:, 4 + u % 2, :]
                    neg = small[:, 4 * (u % 2):4 * (u % 2) + 2]
                    if biased:
                        landed = 32 * (u // 2 + 1) if kind == "moba" else 128 + 64 * ((u - u0) // 2 + 1)
                        dve.wait_ge(bias_landed[u % 2], landed)
                        b = bias[:, u % 2, :]
                        if kind == "na":
                            b3 = b.rearrange("p (r c) -> p r c", c=GRID)
                            link(dve.tensor_tensor(b3, b3, const("window").unsqueeze(1).broadcast_to([P, 8, GRID]),
                                                   ALU.add))
                            settle()
                        link(dve.scalar_tensor_tensor(out=logit[:, u % 2, :], in0=src, scalar=scale, in1=b,
                                                      op0=ALU.mult, op1=ALU.add))
                        settle()
                        src = logit[:, u % 2, :]
                    ins = dve.tensor_reduce(neg, src.rearrange("p (q k) -> p q k", q=2), AX_X, ALU.max,
                                            negate=True)
                    if not biased:
                        link(ins)
                        settle()
                        ins = dve.tensor_scalar(neg, neg, scale, None, ALU.mult)
                    ins.then_inc(max_ready, 1)

                def back(u):
                    dve.wait_ge(exp_done, u + 1)
                    r = small[:, 32 + 2 * (u % 2):34 + 2 * (u % 2)]
                    link(dve.reciprocal(r, small[:, 8 + 4 * (u % 2):10 + 4 * (u % 2)]))
                    settle()
                    for qt in range(2):
                        o = prob[:, u % 2, qt * S:(qt + 1) * S]
                        ins = dve.tensor_scalar(o, o, r[:, qt:qt + 1], None, ALU.mult)
                    ins.then_inc(p_ready, 1)

                front(u0)
                for u in range(u0, u0 + n):
                    if u + 1 < u0 + n:
                        front(u + 1)
                    back(u)

            dve.memset(tab_rpb, 0.0).then_inc(rpb_zero, 1)
            link(dve.memset(tab_row[:, S:REL], MASKED))
            dve.wait_ge(rel_ps, 1)
            settle()
            dve.tensor_copy(tab_row[:, 0:S], ps[0:8, 5, 0:S]).then_inc(rel_row, 1)
            dve.wait_ge(s_vec, 16)
            for q in range(4):
                dve.wait_ge(s_mem[q], 16)
            memory = region(0, 16)
            norm("mem", lambda c: memory[:, c, :], lambda c: col("mem_g", c))
            dve.wait_ge(c_ready, 1)
            for u in range(8):
                if u == 6:
                    dve.wait_ge(al_ready, 4)
                    newton("mix")
                if u == 4:
                    ada_mod(0)
                ada_unit(u)
            ada_mod(1)

            dve.wait_ge(s_const, 16)
            norm("mix", lambda c: res[:, c, :], lambda c: mod[:, 0, c:c + 1], lambda c: mod[:, 1, c:c + 1],
                 summed=True)
            for g in range(8):
                if g == 7:
                    conv_ssm(6, 0, 0)
                if g == 4:
                    ada_mod(2)
                ada_unit(8 + g)
            conv_ssm(7, 1, 1)
            ada_mod(3)
            conv_ssm(10, 2, 0)
            G = G0["dt"]
            dve.wait_ge(half_used, H0["dt"] + 2)
            for t in range(2):
                ins = dve.tensor_tensor(dts[:, 0, 16 * t:16 * t + 16], acc_tok(G)[:, t, 0:16],
                                        col("dtb", 0, 16), ALU.add)
            ins.then_inc(evac[G % 2], 1)
            dve.wait_ge(evac[G % 2], G // 2 + 1)
            dve.scalar_tensor_tensor(out=dts[:, 1, :], in0=dts[:, 0, :], scalar=-1.0, in1=dts[:, 0, :],
                                     op0=ALU.mult, op1=ALU.min).then_inc(dt_done, 1)
            attention("moba", HD ** -0.5)

            e, s_, z2, p_ = dts[:, 2, :], dts[:, 6, :], dts[:, 7, :], dts[:, 8, :]
            dve.wait_ge(dt_exp, 1)
            link(dve.tensor_scalar(dts[:, 4, :], e, 2.0, None, ALU.add))
            link(dve.tensor_scalar(dts[:, 9, :], dts[:, 0, :], 0.0, None, ALU.max))
            settle()
            link(dve.reciprocal(dts[:, 5, :], dts[:, 4, :]))
            settle()
            link(dve.tensor_tensor(s_, e, dts[:, 5, :], ALU.mult))
            settle()
            link(dve.tensor_tensor(z2, s_, s_, ALU.mult))
            settle()
            link(dve.tensor_scalar(p_, z2, 1.0 / 15, None, ALU.mult))
            for k in (13, 11, 9, 7, 5, 3):
                settle()
                link(dve.scalar_tensor_tensor(out=p_, in0=p_, scalar=1.0 / k, in1=z2, op0=ALU.add,
                                              op1=ALU.mult))
            settle()
            link(dve.scalar_tensor_tensor(out=p_, in0=p_, scalar=1.0, in1=s_, op0=ALU.add, op1=ALU.mult))
            settle()
            link(dve.scalar_tensor_tensor(out=dts[:, 10, :], in0=p_, scalar=2.0, in1=dts[:, 9, :],
                                          op0=ALU.mult, op1=ALU.add))
            settle()
            for t in range(2):
                link(dve.scalar_tensor_tensor(out=dts[:, 11, 16 * t:16 * t + 16],
                                              in0=dts[:, 10, 16 * t:16 * t + 16], scalar=-1.0,
                                              in1=dts[:, 3, 0:16], op0=ALU.mult, op1=ALU.mult))
            settle()

            tri = const("tri")
            dve.wait_ge(gram_ready, 2)
            for g in range(2):
                dve.tensor_tensor(gram[:, g, 0:S], ps[:, 4 + g, 0:S], tri, ALU.mult)
                link(dve.tensor_tensor(gram[:, g, S:S + P], ps[:, 4 + g, S:S + P], tri[:, 0:P], ALU.mult))
            settle()

            def seg(h):
                if h >= 2:
                    dve.wait_ge(seg_summed, h - 1)
                r = seg_in[:, h % 2, :]
                dve.tensor_scalar(r[:, 0:S], tri, dts[:, 11, h:h + 1], None, ALU.mult)
                dve.tensor_scalar(r[:, S:S + P], tri[:, 0:P], dts[:, 11, 16 + h:17 + h], None, ALU.mult)\
                   .then_inc(seg_ready, 1)

            def mixing(h):
                dve.wait_ge(decay_ready, h + 1)
                if h >= 2:
                    dve.wait_ge(y_ready, h - 1)
                for t, (a, b) in enumerate([(0, S), (S, S + P)]):
                    ins = dve.scalar_tensor_tensor(out=mix_m[:, h % 2, a:b], in0=decay[:, h % 2, a:b],
                                                   scalar=dts[:, 10, 16 * t + h:16 * t + h + 1],
                                                   in1=gram[:, h // 8, a:b], op0=ALU.mult, op1=ALU.mult)
                ins.then_inc(m_ready, 1)

            def gate_y(c):
                dve.wait_ge(y_ready, 2 * c + 2)
                o = work[:, 3072 + (c % 2) * S:3072 + (c % 2 + 1) * S]
                link(dve.scalar_tensor_tensor(out=o, in0=xs_r[:, c, :], scalar=col("dskip", c),
                                              in1=head_state(c), op0=ALU.mult, op1=ALU.add))
                settle()
                dve.tensor_tensor(z_r[:, c, :], o, z_r[:, c, :], ALU.mult).then_inc(y_done, 1)

            seg(0)
            seg(1)
            for h in range(STATE_HEADS):
                mixing(h)
                if h + 2 < STATE_HEADS:
                    seg(h + 2)
                if h % 2 == 0 and h:
                    gate_y(h // 2 - 1)
            gate_y(7)
            dve.wait_ge(y_done, 8)

            norm("mixin", lambda c: q_r[:, c, :] if c < 8 else z_r[:, c - 8, :],
                 lambda c: col("attn_g", c) if c < 8 else col("ssm_g", c - 8))
            residual_groups("wout", gate=2, between=lambda g: ada_unit(16 + g))
            ada_mod(4)
            norm("ffn", lambda c: res[:, c, :], lambda c: mod[:, 3, c:c + 1], lambda c: mod[:, 4, c:c + 1])

            def up_conv(g, i=None, extra=None):
                G = G0["up"] + g
                base = H0["up"] + 8 * g + 8
                dve.wait_ge(half_used, base if i is None else i * 16 + base)
                if i is not None:
                    dve.wait_ge(hid_ready, i * 2 + (g - 1))

                def column(name, n, k):
                    if i is None:
                        return col(name, n)
                    return vec[:, bass.ds(i * k + (V0[name] + n), 1)]

                convolve(conv[:, g % 2], acc(G), lambda c, t: column("cf_w", 12 * g + 3 * c + t, 24),
                         lambda c: column("cf_b", 4 * g + c, 8), 3, evac[G % 2], extra)

            def up_gate(g, i=None):
                base = 3 + g + 1
                dve.wait_ge(silu_ready, base if i is None else i * 2 + base)
                o = hidden[:, 2 * g:2 * g + 2, :] if i is None else hidden[:, bass.ds(i * 4 + 2 * g, 2), :]
                dve.tensor_tensor(o, conv[:, g % 2, 0:2, :], conv[:, g % 2, 2:4, :], ALU.mult)\
                   .then_inc(hid_ready, 1)

            def last_slice_rows(i):
                for s in range(4):
                    n = i * 4 + (160 + s)
                    dve.wait_ge(ada_landed[s % 2], i * 32 + 16 * (65 + s // 2))
                    dve.wait_ge(ada_used, n - 1)
                    a = ada_acc[:, s % 2 * 1024:(s % 2 + 1) * 1024]
                    dve.scalar_tensor_tensor(out=a, in0=ada_slot(s % 2),
                                             scalar=small[:, bass.ds(i * 2 + (16 + s // 2), 1)], in1=a,
                                             op0=ALU.mult, op1=ALU.add).then_inc(ada_used, 1)

            dve.wait_ge(ada_summed, 5)
            link(dve.memset(ada_acc, 0.0))
            up_conv(0)
            up_conv(1)
            up_gate(0)
            PER_TURN = 16

            def up_turn(i):
                for p in range(2):
                    up_conv(2 + p, i, i * PER_TURN)
                    up_gate(1 + p, i)

            before = steps[0]
            with dve.Fori(0, 8) as i:
                last_slice_rows(i)
                up_turn(i)
            assert steps[0] - before == PER_TURN
            steps[0] = before
            with dve.Fori(8, 10) as i:
                up_turn(i)
            steps[0] = before + 10 * PER_TURN
            up_gate(21)
            ada_mod(5)
            down("down", 0, gate=5)

            norm_in_place("fin", lambda c: col("fin_g", c), res_ready)
            dve.wait_ge(res_ready, 4)
            norm("lnmix", lambda c: res[:, c, :], lambda c: col("lnmix_g", c))
            attention("na", HD ** -0.5)
            for q in range(2):
                G = G0["win2"] + 6 + q
                dve.wait_ge(evac[G % 2], G // 2 + 1)
            dve.wait_ge(o_evac, 16)
            norm("qkv", lambda c: ckv_r[:, c, :], lambda c: col("q_g", c) if c < 4 else col("kv_g", c - 4))

            G = G0["uq"] + 2
            dve.wait_ge(evac[G % 2], G // 2 + 1)
            for j, c in enumerate([0, 1, 2, 3, 6]):
                dve.wait_ge(rot_ready, j + 1)
                o = work[:, 3584:3584 + S]
                link(dve.tensor_tensor(o, ps[:, 5, 0:S], const("sin"), ALU.mult))
                link(dve.tensor_tensor(ckv_r[:, c, :], ckv_r[:, c, :], const("cos"), ALU.mult))
                settle()
                dve.tensor_tensor(ckv_r[:, c, :], ckv_r[:, c, :], o, ALU.add).then_inc(rot_done, 1)
                dve.wait_ge(rot_done, j + 1)
            attention("mla", 192 ** -0.5)
            dve.wait_ge(o_evac, 24)
            norm("mixin2", lambda c: q_r[:, c, :] if c < 8 else qn_r[:, c - 8, :],
                 lambda c: col("na_g", c) if c < 8 else col("mla_g", c - 8))
            residual_groups("wout2")
            for g in range(4):
                G = G0["wout2"] + g
                dve.wait_ge(evac[G % 2], G // 2 + 1)
            norm("lnmem", lambda c: res[:, c, :], lambda c: col("lnmem_g", c))
            attention("x", 512 ** -0.5)
            for q in range(4):
                dve.wait_ge(ah_ready, al_before("xo") + q + 1)
                dve.tensor_tensor(a_lo[:, 4 * q:4 * q + 4, :], qx_r[:, 4 * q:4 * q + 4, :],
                                  a_hi[:, 4 * q:4 * q + 4, :].bitcast(F32), ALU.subtract)\
                   .then_inc(al_ready, 1)
            residual_groups("xo")
            for g in range(4):
                G = G0["xo"] + g
                dve.wait_ge(evac[G % 2], G // 2 + 1)
            norm("lnffn", lambda c: res[:, c, :], lambda c: col("lnffn_g", c))

            def swiglu(g, i=None):
                G, base = G0["gu"] + g, 25 + g + 1
                dve.wait_ge(silu_ready, base if i is None else i * 2 + base)
                o = hidden[:, 2 * g:2 * g + 2, :] if i is None else hidden[:, bass.ds(i * 4 + 2 * g, 2), :]
                dve.tensor_tensor(o, acc(G)[:, 2:4, :], conv[:, g % 2, 0:2, :], ALU.mult)\
                   .then_inc(evac[G % 2], 1)

            swiglu(0)
            with dve.Fori(0, 10) as i:
                for p in range(2):
                    swiglu(1 + p, i)
            swiglu(21)
            down("down2", 22)
            norm_in_place("fin2", lambda c: col("fin2_g", c), out_ready)


def _tiles(w, cols=512, chunks=4):
    k, n = w.shape
    w = w.reshape(k // (P * chunks), chunks, P, n // cols, cols)
    return w.transpose(3, 0, 2, 1, 4).reshape(-1, P, chunks * cols)


def _down_tiles(w):
    w = w.reshape(11, 4, P, 2, 2, 512)
    return w.transpose(3, 0, 4, 2, 1, 5).reshape(-1, P, TILE)


def _pairs(gate, value):
    k = gate.shape[0]
    both = np.stack([gate.reshape(k, -1, 256), value.reshape(k, -1, 256)], axis=2)
    return both.reshape(k, -1)


def _cols(v, width=P):
    return np.asarray(v).reshape(-1, width).T


def _constants():
    p = np.arange(P)
    tri = (p[:, None] <= np.arange(S)[None, :]).astype(np.float32)
    after = (p[:, None] > p[None, :]).astype(np.float32)
    ident = np.eye(P, dtype=np.float32)
    inv = (1.0 / (np.float32(10000.0) ** (np.arange(0, 64, 2, dtype=np.float32) / np.float32(64)))).astype(np.float32)
    ang = np.arange(S, dtype=np.float32)[None, :] * inv[:, None]
    cos, sin = np.tile(np.cos(ang), (4, 1)), np.tile(np.sin(ang), (4, 1))
    rot = np.zeros((P, P), np.float32)
    for m in range(P):
        if m % 64 < 32:
            rot[m + 32, m] = -1.0
        else:
            rot[m - 32, m] = 1.0
    c = p % GRID
    start = np.clip(c - 8, 0, GRID - 16)
    k = np.arange(GRID)[None, :]
    window = np.where((k >= start[:, None]) & (k < start[:, None] + 16), 0.0, MASKED)
    consts = np.concatenate([tri, after, ident, cos, sin, rot, window], axis=1).astype(np.float32)
    dist = 255 - np.arange(S)
    nf = np.maximum(dist, 16).astype(np.float32)
    large = 16 + (np.log(nf / np.float32(16)) / np.float32(np.log(8.0)) * np.float32(16)).astype(np.int32)
    bucket = np.where(dist < 16, dist, np.minimum(large, 31))
    onehot = np.zeros((32, 512), np.float32)
    onehot[bucket, np.arange(S)] = 1.0
    return consts, onehot


def _layout(a):
    w_in = a["w_in"][0]
    dt = np.zeros((P, TILE), np.float32)
    dt[:, 0:256] = w_in[:, 5632:5648].reshape(16, P, 16).transpose(1, 0, 2).reshape(P, 256)
    w_in2 = a["w_in_2"][0]
    rope = w_in2[:, 3840:3904]
    w_in2 = np.concatenate([w_in2[:, 0:3840], rope, rope, rope, rope], axis=1)
    uq = a["w_uq_2"][0].reshape(512, NH, 192)
    uq = np.concatenate([uq[:, :, 0:128].reshape(512, -1), uq[:, :, 128:].reshape(512, -1)], axis=1)
    ukv = a["w_ukv_2"][0].reshape(256, NH, 256)
    ukv = np.concatenate([ukv[:, :, 0:128].reshape(256, -1), ukv[:, :, 128:].reshape(256, -1)], axis=1)
    ukv = _tiles(ukv, 512, 2).reshape(2, 2, P, HALF).transpose(0, 2, 1, 3).reshape(2, P, TILE)
    up = a["w_up"][0]
    stream = np.concatenate([
        _tiles(a["w_xk_2"][0]), _tiles(w_in[:, 0:5632]), dt[None], _tiles(a["w_xv_2"][0]),
        _tiles(a["w_out"][0]), _tiles(_pairs(up[:, :FF], up[:, FF:])), _down_tiles(a["w_down"][0]),
        _tiles(w_in2), _tiles(uq), ukv, _tiles(a["w_out_2"][0]), _tiles(a["w_xq_2"][0]),
        _tiles(a["w_xo_2"][0]), _tiles(_pairs(a["w_gate_2"][0], a["w_up_2"][0])),
        _down_tiles(a["w_down_2"][0])])
    ada = a["w_ada"][0].reshape(16, P, 6, 2, 1024)[:, :, ADA_ORDER]
    ada = ada.transpose(2, 0, 3, 1, 4).reshape(-1, P, 1024)
    cw, cb = a["conv_ffn_w"][0], a["conv_ffn_b"][0]
    cfw = _pairs(cw[:, :FF], cw[:, FF:]).reshape(3, 88, P).transpose(2, 1, 0).reshape(P, 264)
    cfb = _cols(_pairs(cb[None, :FF], cb[None, FF:]))
    csw = a["conv_ssm_w"][0].reshape(4, 12, P).transpose(2, 1, 0).reshape(P, 48)
    parts = {"c": _cols(a["c"][0]), "b_ada": _cols(a["b_ada"][0]), "mix_g": _cols(a["norm_mix_g"][0]),
             "attn_g": _cols(a["attn_norm_g"][0]), "ssm_g": _cols(a["ssm_norm_g"][0]), "cs_w": csw,
             "cs_b": _cols(a["conv_ssm_b"][0]), "dskip": _cols(np.repeat(a["d_skip"][0], 64)),
             "ffn_g": _cols(a["norm_ffn_g"][0]), "cf_b": cfb, "cf_w": cfw,
             "fin_g": _cols(a["final_norm_g"]), "lnmix_g": _cols(a["ln_mix_2"][0]),
             "q_g": _cols(a["q_norm_2"][0]), "kv_g": _cols(a["kv_norm_2"][0]),
             "na_g": _cols(a["na_out_norm_2"][0]), "mla_g": _cols(a["mla_out_norm_2"][0]),
             "lnmem_g": _cols(a["ln_mem_2"][0]), "mem_g": _cols(a["mem_norm_2"][0]),
             "lnffn_g": _cols(a["ln_ffn_2"][0]), "fin2_g": _cols(a["final_norm_2"]),
             "dtb": np.tile(a["dt_bias"][0], (P, 1)), "alog": np.tile(a["a_log"][0], (P, 1))}
    vecs = np.concatenate([parts[n] for n, _ in VEC], axis=1)
    assert vecs.shape == (P, NVEC)
    turned = lambda x: x[0].T.reshape(16, P, S).transpose(1, 0, 2)
    consts, onehot = _constants()
    return {"stream": stream, "ada": ada, "xT": turned(a["x"]), "memT": turned(a["mem_2"]), "vecs": vecs,
            "consts": consts, "onehot": onehot, "relb": a["rel_bias"],
            "rpb": a["na_rpb_2"][0][:, 4:11].reshape(56, 31)}


def kernel(**inputs):
    import concourse.bacc as _bacc
    from concourse.bass_utils import run_bass_kernel_spmd as _run

    a = {k: np.asarray(v) for k, v in inputs.items()}
    arrays = {k: np.ascontiguousarray(v) for k, v in _layout(a).items()}
    nc = _bacc.Bacc("TRN2", target_bir_lowering=False, num_devices=1)
    args = [nc.dram_tensor(k, v.shape, F32, kind="ExternalInput").ap() for k, v in arrays.items()]
    out = nc.dram_tensor("out", [P, 16, S], F32, kind="ExternalOutput").ap()
    scratch = [nc.dram_tensor(n, s, F32).ap() for n, s in
               [("rel_rows", [8, P, REL]), ("rpb_rows", [56, GRID, NA_W]), ("k_spill", [4, P, 1024]),
                ("v_spill", [4, P, 1024])]]
    scratch += [nc.dram_tensor(n, [P, 16, S], F32).ap() for n in ("mem_high", "mem_low")]
    block_program(nc, *args, out, *scratch)
    r = _run(nc, [arrays], core_ids=[0])
    got = r.results[0]["out"]
    return got.transpose(1, 0, 2).reshape(D, S).T.reshape(1, S, D)
```
